# Optimizing a Trainium2 kernel written in Bass

```python
import math
import jax, jax.numpy as jnp
from jax import lax
import numpy as np

D_MODEL = 1024
BATCH = 1
SEQ = 512
DEPTH = 1

CHUNK = 64
CONV_DIM = D_MODEL // 2
CONV_WIDTH = 31
N_HEADS = 8
HEAD_DIM = 64
ATT_DIM = N_HEADS * HEAD_DIM
QBLOCK = 128
D_FF = ((8 * D_MODEL + 3 * 256 - 1) // (3 * 256)) * 256
EPS = 1e-6
IN_COLS = 2 * CONV_DIM + 3 * ATT_DIM + 2 * D_MODEL


def rmsnorm(x, g):
    xf = x.astype(jnp.float32)
    y = xf * lax.rsqrt(jnp.mean(xf * xf, axis=-1, keepdims=True) + EPS)
    return (y * g.astype(jnp.float32)).astype(x.dtype)

def layernorm(x, g, b):
    xf = x.astype(jnp.float32)
    mu = jnp.mean(xf, axis=-1, keepdims=True)
    var = jnp.mean(jnp.square(xf - mu), axis=-1, keepdims=True)
    y = (xf - mu) * lax.rsqrt(var + EPS)
    return (y * g.astype(jnp.float32) + b.astype(jnp.float32)).astype(x.dtype)

def causal_depthwise_conv(u, w, b):
    k, c = w.shape
    up = jnp.pad(u, ((0, 0), (k - 1, 0), (0, 0)))
    y = lax.conv_general_dilated(
        up, w[:, None, :].astype(u.dtype), window_strides=(1,), padding='VALID',
        dimension_numbers=('NWC', 'WIO', 'NWC'), feature_group_count=c)
    return y + b.astype(u.dtype)

def stick_breaking_attention(q, k, v):
    s_len = q.shape[1]
    scale = 1.0 / math.sqrt(q.shape[-1])
    outs = []
    for i in range(s_len // QBLOCK):
        q0 = i * QBLOCK
        q1 = q0 + QBLOCK
        qb = q[:, q0:q1].astype(jnp.float32)
        kb = k[:, :q1].astype(jnp.float32)
        vb = v[:, :q1].astype(jnp.float32)
        z = jnp.einsum('bqhd,bkhd->bhqk', qb, kb) * scale
        t_idx = q0 + jnp.arange(QBLOCK)[:, None]
        s_idx = jnp.arange(q1)[None, :]
        mask = s_idx < t_idx
        log_1m = jnp.where(mask, jax.nn.log_sigmoid(-z), 0.0)
        rev_excl = lax.cumsum(log_1m, axis=3, reverse=True) - log_1m
        a = jnp.where(mask, jnp.exp(jax.nn.log_sigmoid(z) + rev_excl), 0.0)
        outs.append(jnp.einsum('bhqk,bkhd->bqhd', a, vb))
    return jnp.concatenate(outs, axis=1).astype(q.dtype)

def first_inputs(seed: int = 0) -> dict:
    key = jax.random.key(seed)
    ks = jax.random.split(key, 20)
    f32 = jnp.float32

    def w(k, shape, fan_in):
        return jax.random.normal(k, shape, f32) * (fan_in ** -0.5)

    def gain(k, n):
        return 1.0 + 0.05 * jax.random.normal(k, (n,), f32)

    def bias(k, n):
        return 0.02 * jax.random.normal(k, (n,), f32)

    return {
        'x': jax.random.normal(ks[0], (BATCH, SEQ, D_MODEL), f32),
        'norm_mix_pre': gain(ks[1], D_MODEL),
        'w_in': w(ks[2], (D_MODEL, IN_COLS), D_MODEL),
        'conv_dw_w': w(ks[3], (CONV_WIDTH, CONV_DIM), CONV_WIDTH),
        'conv_dw_b': bias(ks[4], CONV_DIM),
        'conv_ln_g': gain(ks[5], CONV_DIM),
        'conv_ln_b': bias(ks[6], CONV_DIM),
        'w_conv_branch': w(ks[7], (CONV_DIM, D_MODEL), CONV_DIM),
        'b_conv_branch': bias(ks[8], D_MODEL),
        'w_att_branch': w(ks[9], (ATT_DIM, D_MODEL), ATT_DIM),
        'w_out': w(ks[10], (D_MODEL, D_MODEL), D_MODEL),
        'norm_mix_post': gain(ks[11], D_MODEL),
        'norm_ffn_pre': gain(ks[12], D_MODEL),
        'w_ffn_up': w(ks[13], (D_MODEL, 2 * D_FF), D_MODEL),
        'w_ffn_down': w(ks[14], (D_FF, D_MODEL), D_FF),
        'norm_ffn_post': gain(ks[15], D_MODEL),
    }

def first_block(x, norm_mix_pre, w_in, conv_dw_w, conv_dw_b, conv_ln_g, conv_ln_b,
              w_conv_branch, b_conv_branch, w_att_branch, w_out, norm_mix_post,
              norm_ffn_pre, w_ffn_up, w_ffn_down, norm_ffn_post):
    b, s, d = x.shape
    for _ in range(DEPTH):
        h = rmsnorm(x, norm_mix_pre)
        proj = jnp.einsum('bsd,de->bse', h, w_in)
        splits = np.cumsum([2 * CONV_DIM, ATT_DIM, ATT_DIM, ATT_DIM, D_MODEL]).tolist()
        conv_in, q, k, v, g_conv, g_att = jnp.split(proj, splits, axis=-1)

        u = jax.nn.glu(conv_in, axis=-1)
        u = causal_depthwise_conv(u, conv_dw_w, conv_dw_b)
        u = jax.nn.silu(layernorm(u, conv_ln_g, conv_ln_b))
        conv_out = jnp.einsum('bsc,cd->bsd', u, w_conv_branch) + b_conv_branch

        q = q.reshape(b, s, N_HEADS, HEAD_DIM)
        k = k.reshape(b, s, N_HEADS, HEAD_DIM)
        v = v.reshape(b, s, N_HEADS, HEAD_DIM)
        att = stick_breaking_attention(q, k, v).reshape(b, s, ATT_DIM)
        att_out = jnp.einsum('bsc,cd->bsd', att, w_att_branch)

        merged = jax.nn.sigmoid(g_conv) * conv_out + jax.nn.sigmoid(g_att) * att_out
        mix = jnp.einsum('bsd,de->bse', merged, w_out)
        x = x + rmsnorm(mix, norm_mix_post)

        h = rmsnorm(x, norm_ffn_pre)
        gu = jnp.einsum('bsd,df->bsf', h, w_ffn_up)
        gate, up = jnp.split(gu, 2, axis=-1)
        ff = jnp.einsum('bsf,fd->bsd', jax.nn.silu(gate) * up, w_ffn_down)
        x = x + rmsnorm(ff, norm_ffn_post)
    return x


MOBA_HEADS = D_MODEL // 128
MOBA_WIDTH = MOBA_HEADS * HEAD_DIM
DIFF_HEADS = D_MODEL // 256
DIFF_QK_WIDTH = DIFF_HEADS * 2 * HEAD_DIM
DIFF_VDIM = 2 * HEAD_DIM
DIFF_WIDTH = DIFF_HEADS * DIFF_VDIM
MIX_WIDTH = MOBA_WIDTH + DIFF_WIDTH
IN_WIDTH = 4 * MOBA_WIDTH + 2 * DIFF_QK_WIDTH + 2 * DIFF_WIDTH
MOBA_BLOCK = 256
MOBA_TOPK = 3
MOBA_QCHUNK = 32
DIFF_QBLOCK = 128
NORM_EPS = 1e-6
NEG_INF = -1e30


def rms_norm(x, g):
    xf = x.astype(jnp.float32)
    y = xf * lax.rsqrt(jnp.mean(xf * xf, axis=-1, keepdims=True) + NORM_EPS)
    return (y * g.astype(jnp.float32)).astype(x.dtype)

def alibi_slopes(n_heads):
    return jnp.asarray(2.0 ** (-8.0 * np.arange(1, n_heads + 1) / n_heads), dtype=jnp.float32)

def moba_attention(q, k, v, slopes):
    B, H, S, dh = q.shape
    nb = S // MOBA_BLOCK
    kb = k.reshape(B, H, nb, MOBA_BLOCK, dh)
    vb = v.reshape(B, H, nb, MOBA_BLOCK, dh)
    scale = dh ** -0.5
    topk = min(MOBA_TOPK, nb - 1)
    q_blk = jnp.arange(S) // MOBA_BLOCK
    if topk > 0:
        k_mean = jnp.mean(kb.astype(jnp.float32), axis=3)
        gate = jnp.einsum('bhsd,bhnd->bhsn', q.astype(jnp.float32), k_mean)
        past = jnp.arange(nb)[None, :] < q_blk[:, None]
        gate = jnp.where(past[None, None], gate, NEG_INF)
        _, sel_idx = lax.top_k(gate, topk)
    bi = jnp.arange(B)[:, None, None, None]
    hi = jnp.arange(H)[None, :, None, None]
    slope4 = slopes[None, :, None, None]

    def chunk(c):
        t0 = c * MOBA_QCHUNK
        qc = lax.dynamic_slice_in_dim(q, t0, MOBA_QCHUNK, axis=2)
        tq = t0 + jnp.arange(MOBA_QCHUNK)
        own = t0 // MOBA_BLOCK
        k_own = lax.dynamic_index_in_dim(kb, own, axis=2, keepdims=False)
        v_own = lax.dynamic_index_in_dim(vb, own, axis=2, keepdims=False)
        s_own = own * MOBA_BLOCK + jnp.arange(MOBA_BLOCK)
        dist_own = (tq[:, None] - s_own[None, :]).astype(jnp.float32)
        sc_own = jnp.einsum('bhqd,bhkd->bhqk', qc, k_own).astype(jnp.float32) * scale - slope4 * dist_own
        sc_own = jnp.where((s_own[None, :] <= tq[:, None])[None, None], sc_own, NEG_INF)
        if topk == 0:
            p = jax.nn.softmax(sc_own, axis=-1)
            return jnp.einsum('bhqk,bhkd->bhqd', p.astype(v.dtype), v_own)
        ic = lax.dynamic_slice_in_dim(sel_idx, t0, MOBA_QCHUNK, axis=2)
        k_sel = kb[bi, hi, ic]
        v_sel = vb[bi, hi, ic]
        s_sel = ic[..., None] * MOBA_BLOCK + jnp.arange(MOBA_BLOCK)
        dist_sel = (tq[None, None, :, None, None] - s_sel).astype(jnp.float32)
        sc_sel = jnp.einsum('bhqd,bhqjkd->bhqjk', qc, k_sel).astype(jnp.float32) * scale
        sc_sel = sc_sel - slopes[None, :, None, None, None] * dist_sel
        sc_sel = jnp.where((ic < own)[..., None], sc_sel, NEG_INF)
        n_sel = topk * MOBA_BLOCK
        scores = jnp.concatenate([sc_sel.reshape(B, H, MOBA_QCHUNK, n_sel), sc_own], axis=-1)
        p = jax.nn.softmax(scores, axis=-1).astype(v.dtype)
        out = jnp.einsum('bhqk,bhqkd->bhqd', p[..., :n_sel],
                         v_sel.reshape(B, H, MOBA_QCHUNK, n_sel, dh))
        return out + jnp.einsum('bhqk,bhkd->bhqd', p[..., n_sel:], v_own)

    outs = lax.map(chunk, jnp.arange(S // MOBA_QCHUNK))
    return outs.transpose(1, 2, 0, 3, 4).reshape(B, H, S, dh)

def diff_attention(q, k, v, lam, slopes):
    B, H, S, _, dh = q.shape
    scale = dh ** -0.5
    sk = jnp.arange(S)
    slope5 = slopes[None, :, None, None, None]

    def block(c):
        t0 = c * DIFF_QBLOCK
        qc = lax.dynamic_slice_in_dim(q, t0, DIFF_QBLOCK, axis=2)
        tq = t0 + jnp.arange(DIFF_QBLOCK)
        sc = jnp.einsum('bhqcd,bhkcd->bhcqk', qc, k).astype(jnp.float32) * scale
        dist = (tq[:, None] - sk[None, :]).astype(jnp.float32)
        sc = jnp.where((sk[None, :] <= tq[:, None])[None, None, None], sc - slope5 * dist, NEG_INF)
        p = jax.nn.softmax(sc, axis=-1)
        a = p[:, :, 0] - lam * p[:, :, 1]
        return jnp.einsum('bhqk,bhkd->bhqd', a.astype(v.dtype), v)

    outs = lax.map(block, jnp.arange(S // DIFF_QBLOCK))
    return outs.transpose(1, 2, 0, 3, 4).reshape(B, H, S, v.shape[-1])

def second_inputs(seed: int = 0) -> dict:
    key = jax.random.key(seed)
    ks = jax.random.split(key, 13)
    f32 = jnp.float32
    nrm = lambda k, shape: jax.random.normal(k, shape, dtype=f32)
    return {
        "x": nrm(ks[0], (BATCH, SEQ, D_MODEL)),
        "norm_g": 1.0 + 0.02 * nrm(ks[1], (DEPTH, D_MODEL)),
        "w_in": nrm(ks[2], (DEPTH, D_MODEL, IN_WIDTH)) * D_MODEL ** -0.5,
        "moba_q_norm": 1.0 + 0.02 * nrm(ks[3], (DEPTH, HEAD_DIM)),
        "moba_k_norm": 1.0 + 0.02 * nrm(ks[4], (DEPTH, HEAD_DIM)),
        "diff_q_norm": 1.0 + 0.02 * nrm(ks[5], (DEPTH, HEAD_DIM)),
        "diff_k_norm": 1.0 + 0.02 * nrm(ks[6], (DEPTH, HEAD_DIM)),
        "lambda_q1": 0.1 * nrm(ks[7], (DEPTH, HEAD_DIM)),
        "lambda_k1": 0.1 * nrm(ks[8], (DEPTH, HEAD_DIM)),
        "lambda_q2": 0.1 * nrm(ks[9], (DEPTH, HEAD_DIM)),
        "lambda_k2": 0.1 * nrm(ks[10], (DEPTH, HEAD_DIM)),
        "diff_subln": 1.0 + 0.02 * nrm(ks[11], (DEPTH, DIFF_VDIM)),
        "w_out": nrm(ks[12], (DEPTH, MIX_WIDTH, D_MODEL)) * MIX_WIDTH ** -0.5,
    }

def second_block(x, norm_g, w_in, moba_q_norm, moba_k_norm, diff_q_norm, diff_k_norm,
              lambda_q1, lambda_k1, lambda_q2, lambda_k2, diff_subln, w_out):
    B, S, _ = x.shape
    s_pad = -(-S // MOBA_BLOCK) * MOBA_BLOCK
    moba_slopes = alibi_slopes(MOBA_HEADS)
    diff_slopes = alibi_slopes(DIFF_HEADS)
    split_at = list(np.cumsum([MOBA_WIDTH] * 4 + [DIFF_QK_WIDTH, DIFF_QK_WIDTH, DIFF_WIDTH])) 
    for layer in range(DEPTH):
        h = rms_norm(x, norm_g[layer])
        proj = jnp.einsum('bsd,de->bse', h, w_in[layer])
        proj = jnp.pad(proj, ((0, 0), (0, s_pad - S), (0, 0)))
        mq, mk, mv, mg, dq, dk, dv, dg = jnp.split(proj, split_at, axis=-1)

        to_heads = lambda t: t.reshape(B, s_pad, MOBA_HEADS, HEAD_DIM).transpose(0, 2, 1, 3)
        mq = rms_norm(to_heads(mq), moba_q_norm[layer])
        mk = rms_norm(to_heads(mk), moba_k_norm[layer])
        m_out = moba_attention(mq, mk, to_heads(mv), moba_slopes)
        m_out = m_out.transpose(0, 2, 1, 3).reshape(B, s_pad, MOBA_WIDTH) * jax.nn.silu(mg)

        dq = rms_norm(dq.reshape(B, s_pad, DIFF_HEADS, 2, HEAD_DIM).transpose(0, 2, 1, 3, 4), diff_q_norm[layer])
        dk = rms_norm(dk.reshape(B, s_pad, DIFF_HEADS, 2, HEAD_DIM).transpose(0, 2, 1, 3, 4), diff_k_norm[layer])
        dv = dv.reshape(B, s_pad, DIFF_HEADS, DIFF_VDIM).transpose(0, 2, 1, 3)
        lambda_init = 0.8 - 0.6 * math.exp(-0.3 * layer)
        lam = (jnp.exp(jnp.sum(lambda_q1[layer] * lambda_k1[layer]))
               - jnp.exp(jnp.sum(lambda_q2[layer] * lambda_k2[layer])) + lambda_init)
        d_out = diff_attention(dq, dk, dv, lam, diff_slopes)
        d_out = rms_norm(d_out, diff_subln[layer]) * (1.0 - lambda_init)
        d_out = d_out.transpose(0, 2, 1, 3).reshape(B, s_pad, DIFF_WIDTH) * jax.nn.silu(dg)

        mixed = jnp.concatenate([m_out, d_out], axis=-1)[:, :S]
        x = x + jnp.einsum('bse,ed->bsd', mixed, w_out[layer])
    return x


def setup_inputs(seed=0):
    out = dict(first_inputs(seed))
    for name, value in second_inputs(seed + 1).items():
        if name != "x":
            out[name + "_2"] = value
    return out


def reference(
    x, norm_mix_pre, w_in, conv_dw_w, conv_dw_b, conv_ln_g, conv_ln_b, w_conv_branch,
    b_conv_branch, w_att_branch, w_out, norm_mix_post, norm_ffn_pre, w_ffn_up, w_ffn_down,
    norm_ffn_post, norm_g_2, w_in_2, moba_q_norm_2, moba_k_norm_2, diff_q_norm_2, diff_k_norm_2,
    lambda_q1_2, lambda_k1_2, lambda_q2_2, lambda_k2_2, diff_subln_2, w_out_2,
):
    x = first_block(
        x, norm_mix_pre, w_in, conv_dw_w, conv_dw_b, conv_ln_g, conv_ln_b, w_conv_branch,
        b_conv_branch, w_att_branch, w_out, norm_mix_post, norm_ffn_pre, w_ffn_up, w_ffn_down,
        norm_ffn_post,
    )
    return second_block(
        x, norm_g_2, w_in_2, moba_q_norm_2, moba_k_norm_2, diff_q_norm_2, diff_k_norm_2,
        lambda_q1_2, lambda_k1_2, lambda_q2_2, lambda_k2_2, diff_subln_2, w_out_2,
    )


_drawn_inputs = setup_inputs


def setup_inputs(seed=0):
    import zlib

    import numpy as np

    out = dict(_drawn_inputs(seed))
    spreads = {}
    factors = {'conv_ln_b': 4.366,
     'b_conv_branch': 2.746,
     'norm_g_2': 7.524,
     'moba_q_norm_2': 8.0,
     'moba_k_norm_2': 8.0,
     'diff_q_norm_2': 8.0,
     'diff_k_norm_2': 8.0,
     'lambda_q1_2': 8.0,
     'lambda_k1_2': 6.279,
     'lambda_q2_2': 5.84,
     'lambda_k2_2': 8.0,
     'diff_subln_2': 8.0}
    for name, (base, spread) in spreads.items():
        noise = np.random.default_rng([zlib.crc32(name.encode()), seed]).standard_normal(out[name].shape)
        drawn = base * np.exp(spread * noise) if base else spread * noise
        out[name] = __import__('jax').numpy.asarray(drawn.astype(out[name].dtype))
    for name, factor in factors.items():
        out[name] = (out[name] * factor).astype(out[name].dtype)
    return out
```

```python
from contextlib import ExitStack

import numpy as np

import concourse.bass as bass
from concourse import mybir

F32 = mybir.dt.float32
F32R = mybir.dt.float32r
BF16 = mybir.dt.bfloat16
ALU = mybir.AluOpType
ACT = mybir.ActivationFunctionType
AX = mybir.AxisListType

P = 128
T = 512
D = 1024
KC = D // P
TB = T // P
CONV = 512
CC = CONV // P
TAPS = 31
HALF = T // 2
FF = 2816
FC = FF // P
NEG = -1.0e30
EPS = 1.0e-6
LAMBDA_INIT = 0.2

UNIT = KC * P
U_GLU, U_QK, U_V, U_G = 0, 8, 16, 20
U_BR, U_WO, U_UP, U_DN = 36, 44, 52, 96
U_Q2, U_V2, U_G2, U_W2, UNITS = 120, 136, 144, 152, 160
DN_UNITS = 3
DN_CHUNKS = (8, 8, 6)

T_GLU, T_QK, T_V, T_G, T_WO, T_UP, T_DN, T_Q2, T_V2, T_G2, T_W2 = 0, 8, 16, 20, 36, 44, 88, 96, 112, 120, 128
CREDIT = 4

VEC = {}
_at = 0
for _name, _n in (("g_mix_pre", KC), ("conv_w", CC * TAPS), ("conv_b", CC), ("ln_g", CC), ("ln_b", CC),
                  ("b_branch", KC), ("g_mix_post", KC), ("g_ffn_pre", KC), ("g_ffn_post", KC), ("g_2", KC),
                  ("moba_q", 1), ("moba_k", 1), ("diff_q", 1), ("diff_k", 1), ("subln", 1), ("unused", 3), ("lambdas", 4 * 64)):
    VEC[_name] = _at
    _at += _n
NVEC = _at


class Steps:

    def __init__(self, eng, sem):
        self.eng, self.sem, self.base, self.k, self.i, self.per = eng, sem, 0, 0, None, 0

    def do(self, instruction):
        instruction.then_inc(self.sem, 1)
        self.k += 1
        return instruction

    def wait(self, back=0):
        n = self.base + self.k - back
        self.eng.wait_ge(self.sem, n if self.i is None else self.i * self.per + n)

    def enter(self, i, per, first=0):
        self.i, self.per = i, per
        self.base += self.k - first * per
        self.first, self.k = first, 0

    def leave(self, rounds):
        assert self.k == self.per, f"{self.sem}: {self.k} steps in a round, not {self.per}"
        self.base += self.per * (self.first + rounds)
        self.i, self.k = None, 0


def two_layer_block(nc, xT, vecs, wstream, outT):
    with ExitStack() as ctx:
        at = {}
        top = [-(-nc.sbuf_base // 64) * 64]

        def place(name, shape, dt, offset=None):
            size = int(np.prod(shape[1:])) * (2 if dt == BF16 else 4)
            if offset is None:
                offset = top[0]
                top[0] += -(-size // 64) * 64
            at[name] = offset
            return nc.alloc_sbuf_tensor_at(name, shape, dt, offset=offset)

        def sem(name):
            return ctx.enter_context(nc.semaphore(name))

        resid = place("resid", [P, KC, T], F32)
        a_hi = place("a_hi", [P, KC, T], F32R)
        a_lo = place("a_lo", [P, KC, T], F32R)
        b_hi = place("b_hi", [P, KC, T], F32R)
        b_lo = place("b_lo", [P, KC, T], F32R)
        w_raw = place("w_raw", [P, 4, UNIT], F32)
        w_hi = place("w_hi", [P, 2, UNIT], F32R)
        w_lo = place("w_lo", [P, 2, UNIT], F32R)
        vec = place("vec", [P, NVEC], F32)
        ident_bf = place("ident_bf", [P, P], BF16)
        mask_bf = place("mask_bf", [P, P], BF16)
        tri = place("tri", [P, P], F32R)
        neg_ones = place("neg_ones", [P, P], F32R)
        ones = place("ones", [P, P], F32)
        ident = place("ident", [P, P], F32)
        scale_row = place("scale_row", [P, T], F32)
        head_sel = place("head_sel", [P, 62], F32)
        ncol = place("ncol", [P, 4, 4], F32)
        small = place("small", [P, 32], F32)
        lam_prod = place("lam_prod", [P, 2, 64], F32, at["vec"] + 4 * VEC["conv_w"])
        smax = place("smax", [P, 2, 4], F32)
        neg_max = place("neg_max", [P, 2, 4], F32)
        den = place("den", [P, 2, 4], F32)
        rden = place("rden", [P, 2, 4], F32)
        arena = top[0]
        limit = nc.sbuf_usable_end

        def arena_map(start=arena):
            pos = [start]

            def put(name, shape, dt):
                size = int(np.prod(shape[1:])) * (2 if dt == BF16 else 4)
                t = place(name, shape, dt, pos[0])
                pos[0] += -(-size // 64) * 64
                assert pos[0] <= limit, (name, pos[0] - limit)
                return t

            return put

        g_lo8 = place("g_lo8", [P, KC, T], F32, at["resid"])
        v_tok = place("v_tok", [P, TB, CONV], F32, at["b_hi"])
        k_raw = place("k_raw", [P, 4, T], F32, at["b_lo"])
        put = arena_map()
        g_hi8 = put("g_hi8", [P, KC, T], F32)
        q_raw = put("q_raw", [P, 4, T], F32)
        u_pad = put("u_pad", [P, CC, T + TAPS - 1], F32)
        conv_acc = put("conv_acc", [P, CC, T], F32)
        conv_odd = put("conv_odd", [P, HALF], F32)
        q_hi = put("q_hi", [P, T], F32R)
        q_lo = put("q_lo", [P, T], F32R)
        k_hi = put("k_hi", [P, T], F32R)
        k_lo = put("k_lo", [P, T], F32R)
        v_hi = put("v_hi", [P, TB, P], F32R)
        v_lo = put("v_lo", [P, TB, P], F32R)
        WU = (896, 384)
        OU = (0, 896)
        soft = put("soft", [P, 1280], F32)
        sp = put("sp", [P, 1280], F32)
        sp_hi = put("sp_hi", [P, 1280], F32R)
        sp_lo = put("sp_lo", [P, 1280], F32R)
        pa = put("pa", [P, 1280], F32)
        pa_hi = put("pa_hi", [P, 1280], F32R)
        pa_lo = put("pa_lo", [P, 1280], F32R)
        put = arena_map(at["q_hi"])
        glu_a = put("glu_a", [P, 2, T], F32)
        glu_b = put("glu_b", [P, 2, T], F32)
        sq_x = put("sq_x", [P, KC, T], F32)
        tri_f = put("tri_f", [P, P], F32)
        r_exp0 = put("r_exp0", [P, TB, P], F32)
        put = arena_map(at["q_hi"])
        ln_sq = put("ln_sq", [P, CC, T], F32)
        ln_y = put("ln_y", [P, CC, T], F32)
        ln_row = put("ln_row", [P, T], F32)
        r_exp1 = put("r_exp1", [P, TB, P], F32)
        m1 = put("m1", [P, 2, T], F32)
        m2 = put("m2", [P, 2, T], F32)
        merged = put("merged", [P, 2, T], F32)
        put = arena_map(limit // 64 * 64 - 36 * 1024)
        mix = put("mix", [P, KC, T], F32)
        sq_m = put("sq_m", [P, KC, T], F32)
        r_exp2 = put("r_exp2", [P, TB, P], F32)
        put = arena_map()
        h_hi = put("h_hi", [P, FC, T], F32R)
        h_lo = put("h_lo", [P, FC, T], F32R)
        put = arena_map(at["a_hi"])
        up_g = put("up_g", [P, 2, T], F32)
        up_s = put("up_s", [P, 2, T], F32)
        up_u = put("up_u", [P, 2, T], F32)
        up_h = put("up_h", [P, 2, T], F32)
        put = arena_map(at["a_hi"])
        ffo = put("ffo", [P, KC, T], F32)
        sq_f = put("sq_f", [P, KC, T], F32)
        put = arena_map()
        sq_f2 = put("sq_f2", [P, KC, T], F32)
        r_exp3 = put("r_exp3", [P, TB, P], F32)
        put = arena_map()
        y_qk = put("y_qk", [P, 16, T], F32)
        v2_tok = put("v2_tok", [P, TB, 2 * CONV], F32)
        dist = put("dist", [P, T], F32)
        second = arena_map(at["dist"] + 4 * T)
        bias_h = place("bias_h", [P, T], F32, at["vec"] + 4 * VEC["lambdas"])
        assert at["bias_h"] + 4 * T <= at["ones"]
        gate = second("gate", [P, T], F32)
        gate_e = second("gate_e", [P, T], F32)
        q2_hi = second("q2_hi", [P, T], F32R)
        q2_lo = second("q2_lo", [P, T], F32R)
        k2_hi = second("k2_hi", [P, T], F32R)
        k2_lo = second("k2_lo", [P, T], F32R)
        v2_hi = second("v2_hi", [P, TB, P + 64], F32R)
        v2_lo = second("v2_lo", [P, TB, P + 64], F32R)
        s2 = second("s2", [P, 2, 1280], F32)
        pt_hi = second("pt_hi", [P, 1280], F32R)
        pt_lo = second("pt_lo", [P, 1280], F32R)
        put = arena_map(at["w_raw"] + 8 * UNIT)
        att2 = put("att2", [P, T], F32)
        d_sq = put("d_sq", [P, T], F32)
        d_v = put("d_v", [P, T], F32)
        d_y = put("d_y", [P, T], F32)
        put = arena_map(at["gate"])
        sq_q = put("sq_q", [P, 16, T], F32)
        put = arena_map(at["gate"])
        sel_f = put("sel_f", [32, 16, P], F32)
        sel_t = put("sel_t", [32, 16, P], F32R)
        rows_v = put("rows_v", [32, T], F32)
        rows_y = put("rows_y", [32, T], F32)
        rows_t = put("rows_t", [32, T], F32)
        rows_hi = put("rows_hi", [32, T], F32R)
        rows_lo = put("rows_lo", [32, T], F32R)
        out_sb = place("out_sb", [P, KC, T], F32, at["y_qk"])

        ps = ctx.enter_context(nc.psum_tensor("ps", [P, 8, 512], F32))
        psf = ps[:, :, :].rearrange("p b n -> p (b n)")

        vec_loaded, x_again = sem("vec_loaded"), sem("x_again")
        x_loaded = [sem(f"x_loaded{n}") for n in range(2)]
        raw_loaded = [sem(f"raw_loaded{n}") for n in range(4)]
        hi_ready, lo_ready, units_done = sem("hi_ready"), sem("lo_ready"), sem("units_done")
        consts = sem("consts")
        tile_drained, br_drained = sem("tile_drained"), sem("br_drained")
        split_hi, split_lo = sem("split_hi"), sem("split_lo")
        sq_ready, stat_ready, var_ready, std_ready = sem("sq_ready"), sem("stat_ready"), sem("var_ready"), sem("std_ready")
        rexp_ready, row_ready, row_copied = sem("rexp_ready"), sem("row_ready"), sem("row_copied")
        sig_ready = sem("sig_ready")
        vec_step, act_step, pool_step = sem("vec_step"), sem("act_step"), sem("pool_step")
        stage_hi, stage_lo = sem("stage_hi"), sem("stage_lo")
        z_ready, ln_ready, sp_ready = sem("z_ready"), sem("ln_ready"), sem("sp_ready")
        sph_ready, spl_ready, r_ready = sem("sph_ready"), sem("spl_ready"), sem("r_ready")
        exp_done, pah_ready, pal_ready = sem("exp_done"), sem("pah_ready"), sem("pal_ready")
        av_ready, att_hi_done, att_drained = sem("av_ready"), sem("att_hi_done"), sem("att_drained")
        mean_ready, conv_centred, conv_y, conv_act = sem("mean_ready"), sem("conv_centred"), sem("conv_y"), sem("conv_act")
        x_new, sel_ready, dist_ready = sem("x_new"), sem("sel_ready"), sem("dist_ready")
        ssq_ready, rows_var, rows_std, rows_ready = sem("ssq_ready"), sem("rows_var"), sem("rows_std"), sem("rows_ready")
        rows_hi_ready, rows_split = sem("rows_hi_ready"), sem("rows_split")
        nb_ready, nb_used = sem("nb_ready"), sem("nb_used")
        lam_sum, lam_exp = sem("lam_sum"), sem("lam_exp")
        s2_ready, s2_biased, max_ready, p2_exp, p2_norm = (
            sem("s2_ready"), sem("s2_biased"), sem("max_ready"), sem("p2_exp"), sem("p2_norm"))
        qk2_hi, qk2_lo, v2_hi_ready, v2_lo_ready = sem("qk2_hi"), sem("qk2_lo"), sem("v2_hi_ready"), sem("v2_lo_ready")
        pt_ready, pth_ready, ptl_ready, av2_ready = sem("pt_ready"), sem("pth_ready"), sem("ptl_ready"), sem("av2_ready")
        gate_clamped, gate_sig, gate_act = sem("gate_clamped"), sem("gate_sig"), sem("gate_act")
        out_read, raw_copied, dsq_ready, dss_ready, dvar_ready, drs_ready, d_final, att2_final, mixed_ready = (
            sem("out_read"), sem("raw_copied"), sem("dsq_ready"), sem("dss_ready"), sem("dvar_ready"),
            sem("drs_ready"), sem("d_final"), sem("att2_final"), sem("mixed_ready"))
        pool_held, gap_zeroed = sem("pool_held"), sem("gap_zeroed")
        stored = sem("stored")

        block = ctx.enter_context(nc.Block())

        def col(name, j=0, n=1):
            if isinstance(j, int):
                return vec[:, VEC[name] + j:VEC[name] + j + n]
            return vec[:, bass.ds(j + VEC[name], n)]

        def chunk(buf, j):
            if isinstance(j, int):
                return buf[:, j, :]
            return buf[:, bass.ds(j, 1), :].rearrange("p a n -> p (a n)")

        BLOCKS = (((0, 0, 0, 256, None), (1, 0, 256, 256, None), (2, 0, 512, 256, 512), (3, 128, 768, 128, 768)),
                  ((0, 0, 0, 256, 0), (1, 128, 256, 128, 256)))
        S_COL = (896, 1024, 512, 0)
        P_COL = (0, 512, 1024, 896)
        CONSTS = 14

        def tq_of(i, c):
            return i * 3 + (3 * (c // 2) + 2 * (c % 2))

        def chunk_of(i, c):
            return i + (c // 2 + 4 * (c % 2))

        def value_parts(c, buf, src):
            if c % 2:
                return buf[:, :, 0:P], src
            return (buf[:, :, :].rearrange("p b (h f) -> p b h f", f=64)[:, :, 0:3:2, :],
                    src.rearrange("p b (h f) -> p b h f", f=64))

        RAW_BEFORE = U_G2 // 4

        def bank_at(head, half):
            return (2 if head == 0 else 5) if half == 0 else 4

        @block.sync
        def _(sp_eng):
            sp_eng.dma_start(vec[:, :], vecs).then_inc(vec_loaded, 16)
            for n in range(2):
                sp_eng.dma_start(resid[:, 4 * n:4 * n + 4, :], xT[:, 4 * n:4 * n + 4, :]).then_inc(x_loaded[n], 16)
            for k in range(4):
                sp_eng.dma_start(w_raw[:, k, :], wstream[k]).then_inc(raw_loaded[k], 16)

            def load(n4):
                for k in range(4):
                    sp_eng.wait_ge(lo_ready, n4 * 4 + (k - 3))
                    sp_eng.dma_start(w_raw[:, k:k + 1, :],
                                     wstream[bass.ds(n4 * 4 + k, 1)].rearrange("a p n -> p a n")
                                     ).then_inc(raw_loaded[k], 16)

            with sp_eng.Fori(1, U_WO // 4 + 1) as n4:
                load(n4)
            sp_eng.wait_ge(split_lo, 2 * KC + CC)
            sp_eng.dma_start(resid[:, :, :], xT).then_inc(x_again, 16)
            with sp_eng.Fori(U_WO // 4 + 1, U_G2 // 4) as n4:
                load(n4)

            def load_gate(i, m):
                sp_eng.wait_ge(lo_ready, i * 2 + (U_G2 + m - (3 if m < 2 and isinstance(i, int) else 1)))
                sp_eng.dma_start(w_raw[:, m % 2:m % 2 + 1, :],
                                 wstream[bass.ds(i * 2 + (U_G2 + m), 1) if not isinstance(i, int) else
                                         slice(U_G2 + m, U_G2 + m + 1)].rearrange("a p n -> p a n")
                                 ).then_inc(raw_loaded[m % 2], 16)

            load_gate(0, 0)
            load_gate(0, 1)
            with sp_eng.Fori(1, 5) as i:
                load_gate(i, 0)
                load_gate(i, 1)
            sp_eng.wait_ge(mixed_ready, KC)
            for k in (2, 3):
                sp_eng.dma_start(w_raw[:, k, :], wstream[U_W2 + k]).then_inc(raw_loaded[k], 16)
            for k in range(4):
                sp_eng.wait_ge(lo_ready, U_W2 + k + 1)
                sp_eng.dma_start(w_raw[:, k, :], wstream[U_W2 + 4 + k]).then_inc(raw_loaded[k], 16)
            for j in range(KC):
                sp_eng.wait_ge(tile_drained, CREDIT + T_W2 + j + 1)
                sp_eng.dma_start(outT[:, j, :], out_sb[:, j, :]).then_inc(stored, 16)
            sp_eng.wait_ge(stored, 16 * KC)

        @block.tensor
        def _(pe):
            def products(out, s_hi, s_lo, m_hi, m_lo, first=False, last=False):
                pe.matmul(out, s_hi, m_hi, start=first, stop=False, skip_group_check=True)
                pe.matmul(out, s_hi, m_lo, start=False, stop=False, skip_group_check=True)
                return pe.matmul(out, s_lo, m_hi, start=False, stop=last, skip_group_check=True)

            def unit_tile(n, slot, bank, m_hi, m_lo, chunks=KC, at_chunk=0, first=True, last=True, fresh=None, late=None):
                pe.wait_ge(lo_ready, n + 1)
                for c in range(chunks):
                    if fresh is not None:
                        pe.wait_ge(split_lo, fresh + c + 1)
                    if late is not None and c == KC - 1:
                        pe.wait_ge(*late)
                    w = slice(c * P, (c + 1) * P)
                    mm = products(ps[:, bank, :], w_hi[:, slot, w], w_lo[:, slot, w],
                                  m_hi[:, at_chunk + c, :], m_lo[:, at_chunk + c, :],
                                  first=first and c == 0, last=last and c == chunks - 1)
                mm.then_inc(units_done, 1)

            def four_tiles(i, u0, t0, m_hi, m_lo, fresh=None, late=None):
                for k in range(4):
                    pe.wait_ge(tile_drained, i * 4 + (t0 + k + 1))
                    unit_tile(i * 4 + (u0 + k), k % 2, k, m_hi, m_lo, fresh=fresh if k == 0 else None,
                              late=late if k == 0 else None)

            def sums(sq, n_sq, chunks=KC):
                for c in range(chunks):
                    pe.wait_ge(sq_ready, n_sq + c + 1)
                    for b in range(TB):
                        mm = pe.matmul(ps[:, 6, b:b + 1], sq[:, c, b * P:(b + 1) * P], ones[:, 0:1],
                                       start=c == 0 and b == 0, stop=c == chunks - 1, skip_group_check=True)
                mm.then_inc(stat_ready, 1)

            def spread(r_exp, q):
                pe.wait_ge(rexp_ready, q + 1)
                for b in range(TB):
                    mm = pe.matmul(ps[:, 7, b * P:(b + 1) * P], r_exp[:, b, :], ident[:, :], start=True, stop=True)
                mm.then_inc(row_ready, 1)

            def token_tiles(u0, t0):
                pe.wait_ge(tile_drained, CREDIT + t0)
                for u in range(4):
                    pe.wait_ge(lo_ready, u0 + u + 1)
                    for kk in range(2):
                        c = 2 * u + kk
                        for b in range(TB):
                            tok = slice(b * P, (b + 1) * P)
                            w = slice(kk * 512, (kk + 1) * 512)
                            mm = products(ps[:, b, :], a_hi[:, c, tok], a_lo[:, c, tok],
                                          w_hi[:, u % 2, w], w_lo[:, u % 2, w], first=c == 0, last=c == KC - 1)
                    mm.then_inc(units_done, 1)

            pe.sem_inc(z_ready, 4)
            pe.sem_inc(av_ready, 4)
            pe.sem_inc(r_ready, 4)
            pe.sem_inc(s2_ready, 1)
            pe.sem_inc(av2_ready, 1)
            pe.sem_inc(pt_ready, 1)
            pe.wait_ge(consts, CONSTS)

            for k in range(4):
                pe.wait_ge(tile_drained, k + 1)
                unit_tile(k, k % 2, k, a_hi, a_lo, fresh=0 if k == 0 else None)
                if k == 1:
                    sums(sq_x, 0)
                if k == 2:
                    spread(r_exp0, 0)
            with pe.Fori(1, 4) as i:
                four_tiles(i, 0, 0, a_hi, a_lo)
            token_tiles(U_V, T_V)

            def scores(c, head, half, g):
                rows = slice(64 * head, 64 * head + 64)
                pe.wait_ge(exp_done, c * 4 + (g + 3 if half == 1 else g + 1))
                base = bank_at(head, half) * 512
                tok0 = HALF * (1 - half)
                for j, t_in, at_col, width, diag in BLOCKS[half]:
                    out = psf[:, base + at_col:base + at_col + width]
                    tok = slice(tok0 + t_in, tok0 + t_in + width)
                    key = slice(j * P, (j + 1) * P)
                    mm = products(out, k_hi[rows, key], k_lo[rows, key], q_hi[rows, tok], q_lo[rows, tok],
                                  first=at_col in (0, 512))
                    if diag is not None:
                        mm = pe.matmul(psf[:, base + diag:base + diag + P], ident_bf[:, :], mask_bf[:, :],
                                       start=False, stop=False, skip_group_check=True)
                mm.then_inc(z_ready, 1)

            def suffix_sums(c, head, half, g):
                pe.wait_ge(spl_ready, c * 4 + (g + 3))
                base = bank_at(head, half) * 512
                off = OU[half]
                blocks = BLOCKS[half]
                for j, t_in, at_col, width, _ in blocks:
                    for parts in (sp_hi, sp_lo):
                        mm = pe.matmul(psf[:, base + at_col:base + at_col + width], tri[:, :],
                                       parts[:, off + at_col:off + at_col + width],
                                       start=False, stop=False, skip_group_check=True)
                    for j2, t2, at2, width2, _ in blocks[j + 1:]:
                        o = base + at_col + (t2 - t_in)
                        for parts in (sp_hi, sp_lo):
                            mm = pe.matmul(psf[:, o:o + width2], neg_ones[:, :],
                                           parts[:, off + at2:off + at2 + width2],
                                           start=False, stop=False, skip_group_check=True)
                mm.then_inc(r_ready, 1)

            def weighted_values(c, head, half, g):
                if half == 0:
                    pe.wait_ge(att_drained, c * 2 + (head + 1))
                pe.wait_ge(pal_ready, c * 4 + (g + 1))
                off = OU[half]
                tok0 = HALF * (1 - half)
                for j, t_in, at_col, width, _ in BLOCKS[half]:
                    w = slice(off + at_col, off + at_col + width)
                    mm = products(ps[:, 7, tok0 + t_in:tok0 + t_in + width], v_hi[:, j, :], v_lo[:, j, :],
                                  pa_hi[:, w], pa_lo[:, w], first=j == 0)
                mm.then_inc(av_ready, 1)

            def gate_tile(c, k):
                pe.wait_ge(tile_drained, c * 4 + (T_G + k + 3))
                unit_tile(c * 4 + (U_G + k), k % 2, k % 2, a_hi, a_lo)

            with pe.Fori(0, 4) as c:
                gate_tile(c, 0)
                pe.wait_ge(stage_lo, c * 3 + 2)
                scores(c, 0, 0, 0)
                scores(c, 0, 1, 1)
                gate_tile(c, 1)
                scores(c, 1, 0, 2)
                suffix_sums(c, 0, 0, 0)
                suffix_sums(c, 0, 1, 1)
                gate_tile(c, 2)
                scores(c, 1, 1, 3)
                pe.wait_ge(stage_lo, c * 3 + 3)
                weighted_values(c, 0, 0, 0)
                weighted_values(c, 0, 1, 1)
                suffix_sums(c, 1, 0, 2)
                gate_tile(c, 3)
                suffix_sums(c, 1, 1, 3)
                weighted_values(c, 1, 0, 2)
                weighted_values(c, 1, 1, 3)

            pe.wait_ge(conv_centred, 1)
            pe.wait_ge(exp_done, 4 + 16)
            for c in range(CC):
                mm = pe.matmul(ps[:, 2, :], ones[:, :], conv_acc[:, c, :], start=c == 0, stop=c == CC - 1)
            mm.then_inc(mean_ready, 1)
            pe.wait_ge(exp_done, 4 + 16)
            sums(ln_sq, KC, CC)
            pe.wait_ge(att_drained, 1 + 8)
            spread(r_exp1, 1)

            pe.wait_ge(tile_drained, CREDIT + T_WO)
            pe.wait_ge(row_copied, 2)
            pe.wait_ge(split_lo, KC + CC)
            with pe.Fori(0, 2) as i:
                for k in range(4):
                    pe.wait_ge(br_drained, i * 4 + (k + 1))
                    pe.wait_ge(lo_ready, i * 4 + (U_BR + k + 1))
                    for c in range(2 * CC):
                        w = slice(c * P, (c + 1) * P)
                        mm = products(ps[:, k + 4 * (c // CC), :], w_hi[:, k % 2, w], w_lo[:, k % 2, w],
                                      b_hi[:, c, :], b_lo[:, c, :], first=c % CC == 0, last=c % CC == CC - 1)
                    mm.then_inc(units_done, 1)

            pe.wait_ge(br_drained, CREDIT + KC)
            with pe.Fori(0, 2) as i:
                four_tiles(i, U_WO, T_WO, a_hi, a_lo, fresh=KC + CC)
            sums(sq_m, KC + CC)
            spread(r_exp2, 2)
            pe.wait_ge(row_copied, 3)
            for k in range(4):
                pe.wait_ge(tile_drained, T_UP + k + 1)
                unit_tile(U_UP + k, k % 2, k, b_hi, b_lo, fresh=2 * KC + CC if k == 0 else None)
                if k == 0:
                    sums(sq_m, 2 * KC + CC)
                if k == 1:
                    spread(r_exp2, 3)
            with pe.Fori(1, FC // 2) as i:
                four_tiles(i, U_UP, T_UP, b_hi, b_lo)
            pe.wait_ge(split_lo, 3 * KC + CC + 16)
            with pe.Fori(0, 2) as i:
                for k in range(4):
                    pe.wait_ge(tile_drained, i * 4 + (T_DN + k + 1))
                    for r in range(DN_UNITS):
                        if k == 0 and r == 2:
                            pe.wait_ge(split_lo, 3 * KC + CC + FC)
                        m = DN_UNITS * k + r
                        unit_tile(i * 12 + (U_DN + m), m % 2, k, h_hi, h_lo, chunks=DN_CHUNKS[r],
                                  at_chunk=8 * r, first=r == 0, last=r == DN_UNITS - 1)
            sums(sq_f, 3 * KC + CC)
            spread(r_exp3, 4)
            pe.wait_ge(row_copied, 5)

            x2 = 3 * KC + CC + FC
            for k in range(4):
                pe.wait_ge(tile_drained, T_Q2 + k + 1)
                unit_tile(U_Q2 + k, k % 2, k, a_hi, a_lo, fresh=x2 if k == 0 else None)
                if k == 0:
                    sums(sq_f2, 4 * KC + CC)
                if k == 1:
                    spread(r_exp3, 5)
            with pe.Fori(1, 4) as i:
                four_tiles(i, U_Q2, T_Q2, a_hi, a_lo)
            for j in range(16):
                pe.wait_ge(sq_ready, 5 * KC + CC + j + 1)
                mm = pe.matmul(ps[0:32, 4, :], head_sel[:, 30 - 2 * j:62 - 2 * j], sq_q[:, j, :],
                               start=j == 0, stop=j == 15)
            mm.then_inc(ssq_ready, 1)
            token_tiles(U_V2, T_V2)
            pe.wait_ge(rows_split, 1)
            pe.wait_ge(sel_ready, 1)
            pe.wait_ge(row_copied, 6)
            for j in range(16):
                if j >= 2:
                    pe.wait_ge(nb_used, j - 1)
                pe.matmul(ps[:, 6 + j % 2, :], sel_t[:, j, :], rows_hi[:, :], start=True, stop=False)
                pe.matmul(ps[:, 6 + j % 2, :], sel_t[:, j, :], rows_lo[:, :], start=False, stop=True).then_inc(nb_ready, 1)
            token_tiles(U_V2 + 4, T_V2 + 4)
            pe.wait_ge(nb_used, 16)
            pe.wait_ge(tile_drained, CREDIT + T_G2)

            def scores2(i, c, head):
                rows = slice(64 * head, 64 * head + 64)
                if head == 0:
                    pe.wait_ge(qk2_lo, i * 4 + (2 * c + 2))
                pe.wait_ge(s2_biased, i * 16 + (8 * c + 4 * head + 4))
                for b in (3, 2, 0, 1):
                    o = 2 * 512 + S_COL[b]
                    width = (b + 1) * P
                    tok = slice(b * P, (b + 1) * P)
                    mm = products(psf[:, o:o + width], q2_hi[rows, tok], q2_lo[rows, tok],
                                  k2_hi[rows, 0:width], k2_lo[rows, 0:width], first=b != 0)
                mm.then_inc(s2_ready, 1)

            def transposes(i, c, head):
                tq = tq_of(i, c) + head
                pe.wait_ge(p2_norm, tq + 1)
                pe.wait_ge(ptl_ready, tq + 1)
                for j in range(TB):
                    for b in range(j, TB):
                        src = S_COL[b] + j * P
                        o = 5 * 512 + P_COL[j] + (b - j) * P
                        mm = pe.transpose(psf[:, o:o + P], s2[:, head, src:src + P], ident[:, :])
                mm.then_inc(pt_ready, 1)

            def values2(i, c, head):
                tq = tq_of(i, c) + head
                rows = slice(64 * head, 64 * head + P)
                if head == 0:
                    pe.wait_ge(v2_lo_ready, i * 2 + (c + 1))
                    if c % 2 == 0:
                        pe.wait_ge(gap_zeroed, i + (c // 2 + 1))
                    pe.wait_ge(out_read, i * 2 + (c + 1))
                pe.wait_ge(ptl_ready, tq + 2)
                for j in range(TB):
                    width = (TB - j) * P
                    w = slice(P_COL[j], P_COL[j] + width)
                    mm = products(ps[:, 1, j * P:T], v2_hi[:, j, rows], v2_lo[:, j, rows],
                                  pt_hi[:, w], pt_lo[:, w], first=j == 0 and head == 0)
                mm.then_inc(av2_ready, 1)

            def gate_half(i, c, half):
                if half == 0:
                    pe.wait_ge(tile_drained, i * 2 + (CREDIT + T_G2 + c))
                    pe.wait_ge(lo_ready, i * 2 + (U_G2 + c + 1))
                for k in range(4 * half, 4 * half + 4):
                    w = slice(k * P, (k + 1) * P)
                    mm = products(ps[:, 0, :], w_hi[:, c % 2, w], w_lo[:, c % 2, w], a_hi[:, k, :], a_lo[:, k, :],
                                  first=k == 0)
                if half:
                    mm.then_inc(units_done, 1)

            def attention_round(i, c, more=True):
                transposes(i, c, 0)
                gate_half(i, c, 0)
                if more:
                    scores2(i, c + 1, 0)
                values2(i, c, 0)
                if c % 2 == 0:
                    transposes(i, c, 1)
                if more:
                    scores2(i, c + 1, 1)
                gate_half(i, c, 1)
                if c % 2 == 0:
                    values2(i, c, 1)
                else:
                    pe.wait_ge(dsq_ready, i + (c // 2 + 1))
                    pe.matmul(ps[:, 1, :], ones[:, :], d_sq[:, :], start=True, stop=True).then_inc(dss_ready, 1)

            scores2(0, 0, 0)
            scores2(0, 0, 1)
            attention_round(0, 0)
            with pe.Fori(0, 3) as i:
                attention_round(i, 1)
                attention_round(i, 2)
            attention_round(0, 7, more=False)

            pe.wait_ge(mixed_ready, KC - 1)
            pe.wait_ge(tile_drained, CREDIT + T_W2)
            with pe.Fori(0, 2) as i:
                four_tiles(i, U_W2, T_W2, b_hi, b_lo, late=(mixed_ready, KC))

        @block.scalar
        def _(act):
            A = Steps(act, act_step)

            def split_weights(n4, k, width=UNIT):
                act.wait_ge(raw_loaded[k], (n4 + 1) * 16)
                if not (isinstance(n4, int) and n4 * 4 + k < 2):
                    act.wait_ge(units_done, n4 * 4 + (k - 1))
                act.activation(w_hi[:, k % 2, 0:width], w_raw[:, k, 0:width], ACT.Copy).then_inc(hi_ready, 1)

            def ahead(n4, k, width=UNIT):
                split_weights(n4 if k < 2 else n4 + 1, (k + 2) % 4, width)

            def std(q):
                act.wait_ge(var_ready, q + 1)
                act.activation(ncol[:, 1, :], ncol[:, 0, :], ACT.Sqrt).then_inc(std_ready, 1)

            def row(q, dst):
                act.wait_ge(row_ready, q + 1)
                act.activation(dst[:, :], ps[:, 7, :], ACT.Copy).then_inc(row_copied, 1)

            act.sem_inc(exp_done, 4)
            act.wait_ge(vec_loaded, 16)
            for c in range(KC):
                act.wait_ge(x_loaded[c // 4], 16)
                act.activation(a_hi[:, c, :], resid[:, c, :], ACT.Copy, scale=col("g_mix_pre", c)).then_inc(split_hi, 1)
                if c == 3:
                    split_weights(0, 0)
                    split_weights(0, 1)
            for c in range(KC):
                act.activation(sq_x[:, c, :], resid[:, c, :], ACT.Square).then_inc(sq_ready, 1)
            ahead(0, 0)
            std(0)
            ahead(0, 1)
            row(0, scale_row)

            def glu(i, kk):
                act.wait_ge(tile_drained, i * 4 + (CREDIT + 2 * kk + 2))
                act.activation(glu_b[:, kk, :], glu_b[:, kk, :], ACT.Sigmoid).then_inc(sig_ready, 1)

            glu(0, 0)
            ahead(0, 2)
            ahead(0, 3)
            glu(0, 1)
            ahead(1, 0)
            ahead(1, 1)
            glu(1, 0)
            ahead(1, 2)
            ahead(1, 3)
            glu(1, 1)
            with act.Fori(2, 5) as i:
                for k in range(4):
                    ahead(i, k)

            def soft_log(c, head, half, g):
                o = bank_at(head, half) * 512
                w = slice(OU[half], OU[half] + WU[half])
                act.wait_ge(z_ready, c * 4 + (4 + g + 1))
                act.wait_ge(sp_ready, c * 4 + (g + 1))
                A.do(act.activation(soft[:, w], psf[:, o:o + WU[half]], ACT.Abs))
                A.wait()
                A.do(act.activation(soft[:, w], soft[:, w], ACT.Exp, scale=-1.0))
                A.wait()
                act.activation(soft[:, w], soft[:, w], ACT.Ln, bias=1.0).then_inc(ln_ready, 1)

            def soft_high(c, half, g):
                w = slice(OU[half], OU[half] + WU[half])
                act.wait_ge(sp_ready, c * 4 + (2 + g + 1))
                act.wait_ge(r_ready, c * 4 + (g + 3))
                act.activation(sp_hi[:, w], sp[:, w], ACT.Copy).then_inc(sph_ready, 1)

            def probs(c, head, half, g):
                w = slice(OU[half], OU[half] + WU[half])
                bank = (2 if head == 0 else 5) if half == 0 else 4
                act.wait_ge(r_ready, c * 4 + (4 + g + 1))
                act.wait_ge(av_ready, c * 4 + (g + 3))
                act.activation(pa[:, w], psf[:, bank * 512:bank * 512 + WU[half]], ACT.Exp).then_inc(exp_done, 1)
                act.wait_ge(exp_done, c * 4 + (4 + g + 1))
                act.activation(pa_hi[:, w], pa[:, w], ACT.Copy).then_inc(pah_ready, 1)

            def head_out(c, head):
                rows = slice(64 * head, 64 * head + 64)
                act.wait_ge(av_ready, c * 4 + (4 + 2 * head + 2))
                act.activation(b_hi[rows, bass.ds(c + 4, 1), :].rearrange("p a n -> p (a n)"),
                               ps[rows, 7, :], ACT.Copy).then_inc(att_hi_done, 1)

            act.preload_act_table_set("natural_log_exp_and_others")
            with act.Fori(0, 4) as c:
                A.enter(c, 8)
                act.wait_ge(tile_drained, CREDIT + T_G)
                act.wait_ge(z_ready, c * 4 + 4)
                act.activation(q_hi[:, :], chunk(q_raw, c), ACT.Copy, scale=0.125).then_inc(stage_hi, 1)
                act.activation(k_hi[:, :], chunk(k_raw, c), ACT.Copy).then_inc(stage_hi, 1)
                act.wait_ge(av_ready, c * 4 + 4)
                act.activation(v_hi[:, :, :], v_tok[:, :, bass.ds(c * P, P)], ACT.Copy).then_inc(stage_hi, 1)
                ahead(c + 5, 0)
                soft_log(c, 0, 0, 0)
                soft_log(c, 0, 1, 1)
                soft_high(c, 0, 0)
                soft_high(c, 1, 1)
                ahead(c + 5, 1)
                soft_log(c, 1, 0, 2)
                probs(c, 0, 0, 0)
                probs(c, 0, 1, 1)
                soft_high(c, 0, 2)
                ahead(c + 5, 2)
                soft_log(c, 1, 1, 3)
                head_out(c, 0)
                soft_high(c, 1, 3)
                probs(c, 1, 0, 2)
                ahead(c + 5, 3)
                probs(c, 1, 1, 3)
                head_out(c, 1)
            A.leave(4)

            for c in range(CC):
                act.wait_ge(conv_y, c + 1)
                act.activation(ln_sq[:, c, :], conv_acc[:, c, :], ACT.Square).then_inc(sq_ready, 1)
            std(1)
            row(1, ln_row)
            for c in range(CC):
                act.wait_ge(conv_y, CC + c + 1)
                A.do(act.activation(ln_y[:, c, :], ln_y[:, c, :], ACT.Silu, scale=col("ln_g", c), bias=col("ln_b", c)))
            for c in range(CC):
                A.wait(back=CC - 1 - c)
                act.activation(b_hi[:, c, :], ln_y[:, c, :], ACT.Copy).then_inc(split_hi, 1)

            act.preload_act_table(ACT.Sigmoid)
            for c in range(KC):
                act.activation(g_lo8[:, c, :], g_lo8[:, c, :], ACT.Sigmoid).then_inc(sig_ready, 1)
                act.activation(g_hi8[:, c, :], g_hi8[:, c, :], ACT.Sigmoid).then_inc(sig_ready, 1)
            with act.Fori(0, 2) as i:
                for k in range(4):
                    act.wait_ge(x_new, i * 4 + (k + 1))
                    act.activation(chunk(a_hi, i * 4 + k), merged[:, k % 2, :], ACT.Copy).then_inc(split_hi, 1)
                    ahead(i + U_BR // 4, k)

            with act.Fori(0, 2) as i:
                for k in range(4):
                    ahead(i + U_WO // 4, k)
                    act.wait_ge(tile_drained, i * 4 + (CREDIT + T_WO + k + 1))
                    act.activation(chunk(sq_m, i * 4 + k), chunk(mix, i * 4 + k), ACT.Square).then_inc(sq_ready, 1)

            def new_residual(q, n_new, dst, gain, sq):
                std(q)
                row(q, scale_row)
                for c in range(KC):
                    act.wait_ge(x_new, n_new + c + 1)
                    act.activation(dst[:, c, :], resid[:, c, :], ACT.Copy, scale=col(gain, c)).then_inc(split_hi, 1)
                for c in range(KC):
                    act.wait_ge(stat_ready, q + 1)
                    act.activation(sq[:, c, :], resid[:, c, :], ACT.Square).then_inc(sq_ready, 1)

            new_residual(2, KC, b_hi, "g_ffn_pre", sq_m)
            ahead(U_UP // 4, 0)
            std(3)
            ahead(U_UP // 4, 1)
            row(3, scale_row)

            def up_pair(i, kk):
                act.wait_ge(tile_drained, i * 4 + (CREDIT + T_UP + 2 * kk + 1))
                act.activation(up_s[:, kk, :], up_g[:, kk, :], ACT.Silu).then_inc(sig_ready, 1)
                act.wait_ge(x_new, i * 2 + (2 * KC + kk + 1))
                act.activation(chunk(h_hi, i * 2 + kk), up_h[:, kk, :], ACT.Copy).then_inc(split_hi, 1)

            up_pair(0, 0)
            ahead(U_UP // 4, 2)
            ahead(U_UP // 4, 3)
            up_pair(0, 1)
            with act.Fori(1, FC // 2) as i:
                for kk in range(2):
                    ahead(i + U_UP // 4, 2 * kk)
                    ahead(i + U_UP // 4, 2 * kk + 1)
                    up_pair(i, kk)

            with act.Fori(0, 2) as i:
                for k in range(4):
                    for r in range(DN_UNITS):
                        m = DN_UNITS * k + r
                        ahead(i * 3 + (U_DN // 4 + m // 4), m % 4, DN_CHUNKS[(r + 2) % 3] * P)
                    act.wait_ge(tile_drained, i * 4 + (CREDIT + T_DN + k + 1))
                    act.activation(chunk(sq_f, i * 4 + k), chunk(ffo, i * 4 + k), ACT.Square).then_inc(sq_ready, 1)
            new_residual(4, 2 * KC + FC, a_hi, "g_2", sq_f2)
            ahead(U_Q2 // 4, 0)
            std(5)
            ahead(U_Q2 // 4, 1)
            row(5, scale_row)

            def square_q(j, k):
                act.wait_ge(tile_drained, j + (CREDIT + T_Q2 + 1))
                act.activation(chunk(sq_q, j), chunk(y_qk, j), ACT.Square).then_inc(sq_ready, 1)

            act.wait_ge(lam_sum, 1)
            act.activation(small[:, 2:4], small[:, 0:2], ACT.Exp).then_inc(lam_exp, 1)
            square_q(0, 0)
            square_q(1, 1)
            for k in (2, 3):
                ahead(U_Q2 // 4, k)
                square_q(k, k)
            with act.Fori(1, 4) as i:
                for k in range(4):
                    ahead(i + U_Q2 // 4, k)
                    square_q(i * 4 + k, k)
            ahead(U_V2 // 4, 0)
            act.wait_ge(rows_var, 1)
            act.activation(rows_t[:, :], rows_v[:, :], ACT.Sqrt).then_inc(rows_std, 1)
            ahead(U_V2 // 4, 1)
            act.wait_ge(rows_ready, 1)
            act.activation(rows_hi[:, :], rows_y[:, :], ACT.Copy).then_inc(rows_hi_ready, 1)
            for k in range(2, 6):
                ahead(U_V2 // 4 + k // 4, k % 4)

            def split_gate(i, m):
                act.wait_ge(raw_loaded[m % 2], i * 16 + (RAW_BEFORE + m // 2 + 1) * 16)
                act.wait_ge(units_done, i * 2 + (U_G2 + m - 1))
                act.activation(w_hi[:, m % 2, :], w_raw[:, m % 2, :], ACT.Copy).then_inc(hi_ready, 1)

            split_gate(0, 0)
            split_gate(0, 1)
            act.preload_act_table_set("natural_log_exp_and_others")

            def stage_qk(i, c):
                act.wait_ge(s2_ready, i * 4 + (2 * c + 1))
                j = chunk_of(i, c)
                act.activation(q2_hi[:, :], chunk(y_qk, j), ACT.Copy).then_inc(qk2_hi, 1)
                act.activation(k2_hi[:, :], chunk(y_qk, j + 8), ACT.Copy).then_inc(qk2_hi, 1)

            def stage_v(i, c):
                act.wait_ge(av2_ready, tq_of(i, c) + 1)
                j = chunk_of(i, c)
                w = slice(j * P, (j + 1) * P) if isinstance(j, int) else bass.ds(j * P, P)
                dst, src = value_parts(c, v2_hi, v2_tok[:, :, w])
                act.activation(dst, src, ACT.Copy).then_inc(v2_hi_ready, 1)

            def exponentials(i, c, head):
                act.wait_ge(max_ready, i * 4 + (2 * c + head + 1))
                for b in (3, 2, 0, 1):
                    w = slice(S_COL[b], S_COL[b] + (b + 1) * P)
                    e = act.activation(s2[:, head, w], s2[:, head, w], ACT.Exp,
                                       bias=neg_max[:, head, b:b + 1], accum_out=den[:, head, b:b + 1])
                e.then_inc(p2_exp, 1)

            def high_probs(i, c, head):
                tq = tq_of(i, c) + head
                act.wait_ge(pt_ready, tq + 2)
                act.wait_ge(av2_ready, tq + 1)
                act.activation(pt_hi[:, :], psf[:, 5 * 512:5 * 512 + 1280], ACT.Copy).then_inc(pth_ready, 1)

            def gate_sigmoid(i, c):
                act.wait_ge(gate_clamped, i * 2 + (c + 1))
                A.do(act.activation(gate_e[:, :], gate_e[:, :], ACT.Exp, scale=-1.0))
                A.wait()
                A.do(act.activation(gate_e[:, :], gate_e[:, :], ACT.Ln, bias=1.0))
                A.wait()
                act.activation(gate_e[:, :], gate_e[:, :], ACT.Exp, scale=-1.0).then_inc(gate_sig, 1)

            def first_root(i, c):
                act.wait_ge(dvar_ready, i + (c // 2 + 1))
                A.do(act.activation(d_y[:, :], d_v[:, :], ACT.Ln))
                A.wait()
                act.activation(d_y[:, :], d_y[:, :], ACT.Exp, scale=-0.5).then_inc(drs_ready, 1)

            def high_mixed(i, c):
                if c % 2 == 0:
                    act.wait_ge(out_read, i * 2 + (c + 2))
                else:
                    act.wait_ge(att2_final, i + (c // 2 + 1))
                act.activation(chunk(b_hi, chunk_of(i, c)), att2[:, :], ACT.Copy).then_inc(split_hi, 1)

            def act_round(i, c, more=True):
                last = c - 1 if c else None
                if more:
                    stage_qk(i, c + 1)
                stage_v(i, c)
                if last is not None:
                    if last % 2:
                        first_root(i, last)
                    gate_sigmoid(i, last)
                high_probs(i, c, 0)
                if last is not None and last % 2 == 0:
                    high_mixed(i, last)
                if c % 2:
                    act.wait_ge(raw_copied, i + (c // 2 + 1))
                    act.activation(d_sq[:, :], att2[:, :], ACT.Square).then_inc(dsq_ready, 1)
                if more:
                    exponentials(i, c + 1, 0)
                if last is not None and last % 2:
                    high_mixed(i, last)
                if c % 2 == 0:
                    high_probs(i, c, 1)
                if more:
                    exponentials(i, c + 1, 1)
                split_gate(i, c + 2)

            stage_qk(0, 0)
            exponentials(0, 0, 0)
            exponentials(0, 0, 1)
            act_round(0, 0)
            with act.Fori(0, 3) as i:
                A.enter(i, 5)
                act_round(i, 1)
                act_round(i, 2)
            A.leave(3)
            act_round(0, 7, more=False)
            first_root(0, 7)
            gate_sigmoid(0, 7)
            high_mixed(0, 7)

            for m in range(2, 8):
                act.wait_ge(raw_loaded[m % 4], (RAW_BEFORE + m // 4 + (5 if m % 4 < 2 else 1)) * 16)
                act.wait_ge(units_done, U_W2 + m - 1)
                act.activation(w_hi[:, m % 2, :], w_raw[:, m % 4, :], ACT.Copy).then_inc(hi_ready, 1)

        @block.vector
        def _(dve):
            V = Steps(dve, vec_step)

            def ts(out, in0, s1, op0, s2_=None, op1=None):
                if op1 is None:
                    return dve.tensor_scalar(out, in0, s1, None, op0)
                return dve.tensor_scalar(out, in0, s1, s2_, op0, op1)

            def tt(out, in0, in1, op):
                return dve.tensor_tensor(out, in0, in1, op)

            def low(out, in0, high):
                return dve.tensor_tensor(out, in0, high.bitcast(F32), ALU.subtract)

            def low_scaled(out, in0, scale, high):
                return dve.scalar_tensor_tensor(out=out, in0=in0, scalar=scale, in1=high.bitcast(F32),
                                                op0=ALU.mult, op1=ALU.subtract)

            def newton(y, v, t):
                V.do(tt(t, y, y, ALU.mult))
                V.wait()
                V.do(tt(t, t, v, ALU.mult))
                V.wait()
                V.do(ts(t, t, -0.5, ALU.mult, 1.5, ALU.add))
                V.wait()
                V.do(tt(y, y, t, ALU.mult))
                V.wait()

            def norm(q, count, r_exp):
                var, std_, y, t = (ncol[:, n, :] for n in range(4))
                dve.wait_ge(stat_ready, q + 1)
                ts(var, ps[:, 6, 0:TB], 1.0 / count, ALU.mult, EPS, ALU.add).then_inc(var_ready, 1)
                dve.wait_ge(std_ready, q + 1)
                V.do(dve.reciprocal(y, std_))
                V.wait()
                newton(y, var, t)
                dve.tensor_copy(r_exp[:, :, :], ncol[:, 2, :].rearrange("p (b o) -> p b o", o=1).to_broadcast([P, TB, P])
                                ).then_inc(rexp_ready, 1)

            dve.sem_inc(tile_drained, CREDIT)
            dve.sem_inc(br_drained, CREDIT)
            dve.sem_inc(att_drained, 1)
            dve.sem_inc(s2_biased, 4)
            dve.sem_inc(sp_ready, 2)
            dve.sem_inc(out_read, 1)
            dve.sem_inc(ptl_ready, 1)
            for c in range(KC):
                dve.wait_ge(split_hi, c + 1)
                low_scaled(a_lo[:, c, :], resid[:, c, :], col("g_mix_pre", c), a_hi[:, c, :]).then_inc(split_lo, 1)
            norm(0, D, r_exp0)
            dve.wait_ge(row_copied, 1)

            def drain(dst, t, u, bank):
                dve.wait_ge(units_done, u + 1)
                tt(dst, ps[:, bank, :], scale_row[:, :], ALU.mult).then_inc(tile_drained, 1)

            dve.wait_ge(consts, CONSTS)
            for p in range(CC):
                kk = p % 2
                drain(glu_a[:, kk, :], 2 * p, 2 * p, 2 * kk)
                drain(glu_b[:, kk, :], 2 * p + 1, 2 * p + 1, 2 * kk + 1)
                dve.wait_ge(sig_ready, p + 1)
                V.do(tt(u_pad[:, p, TAPS - 1:], glu_a[:, kk, :], glu_b[:, kk, :], ALU.mult))

            def taps(c, half, first, last):
                for k in range(first, last):
                    if isinstance(c, int):
                        src = u_pad[:, c, half * HALF + k:half * HALF + k + HALF]
                        acc = conv_acc[:, c, half * HALF:(half + 1) * HALF]
                    else:
                        src = u_pad[:, bass.ds(c, 1), half * HALF + k:half * HALF + k + HALF].rearrange("p a n -> p (a n)")
                        acc = conv_acc[:, bass.ds(c, 1), half * HALF:(half + 1) * HALF].rearrange("p a n -> p (a n)")
                    w = col("conv_w", c * TAPS + k)
                    if k >= 2:
                        V.wait(back=1)
                    dst = conv_odd[:, :] if k % 2 else acc
                    if k == 0:
                        V.do(ts(dst, src, w, ALU.mult, col("conv_b", c), ALU.add))
                    elif k == 1:
                        V.do(ts(dst, src, w, ALU.mult))
                    else:
                        V.do(dve.scalar_tensor_tensor(out=dst, in0=src, scalar=w, in1=dst, op0=ALU.mult, op1=ALU.add))
                    if k == TAPS - 1:
                        V.wait()
                        V.do(tt(acc, acc, conv_odd[:, :], ALU.add))
                        V.wait()

            def some_taps(first, last):
                for c in range(CC):
                    a, b = max(first - c * TAPS, 0), min(last - c * TAPS, TAPS)
                    if a < b:
                        taps(c, 0, a, b)

            for n in range(8):
                dst = q_raw if n < 4 else k_raw
                drain(dst[:, n % 4, :], T_QK + n, U_QK + n, n % 4)
                V.wait()
                some_taps(11 * n, 11 * n + 11)
            some_taps(88, CC * TAPS)
            for b in range(TB):
                dve.wait_ge(units_done, U_V + 4)
                ts(v_tok[:, b, :], ps[:, b, :], ncol[:, 2, b:b + 1], ALU.mult).then_inc(tile_drained, 1)

            def softplus(c, head, half, g):
                o = bank_at(head, half) * 512
                w = slice(OU[half], OU[half] + WU[half])
                dve.wait_ge(ln_ready, c * 4 + (g + 1))
                dve.wait_ge(spl_ready, c * 4 + (g + 1))
                dve.scalar_tensor_tensor(out=sp[:, w], in0=psf[:, o:o + WU[half]], scalar=0.0, in1=soft[:, w],
                                         op0=ALU.max, op1=ALU.add).then_inc(sp_ready, 1)

            def gate_drain(c, k):
                dst = g_lo8 if k < 2 else g_hi8
                drain(chunk(dst, c * 2 + k % 2), None, c * 4 + (U_G + k), k % 2)

            def head_low(c, head):
                rows = slice(64 * head, 64 * head + 64)
                dve.wait_ge(att_hi_done, c * 2 + (head + 1))
                w = bass.ds(c + 4, 1)
                low(b_lo[rows, w, :].rearrange("p a n -> p (a n)"), ps[rows, 7, :],
                    b_hi[rows, w, :].rearrange("p a n -> p (a n)")).then_inc(att_drained, 1)

            with dve.Fori(0, 4) as c:
                V.enter(c, TAPS + 1)
                dve.wait_ge(stage_hi, c * 3 + 1)
                low_scaled(q_lo[:, :], chunk(q_raw, c), 0.125, q_hi[:, :]).then_inc(stage_lo, 1)
                dve.wait_ge(stage_hi, c * 3 + 2)
                low(k_lo[:, :], chunk(k_raw, c), k_hi[:, :]).then_inc(stage_lo, 1)
                dve.wait_ge(stage_hi, c * 3 + 3)
                low(v_lo[:, :, :], v_tok[:, :, bass.ds(c * P, P)], v_hi[:, :, :]).then_inc(stage_lo, 1)
                gate_drain(c, 0)
                softplus(c, 0, 0, 0)
                softplus(c, 0, 1, 1)
                taps(c, 1, 0, 8)
                gate_drain(c, 1)
                softplus(c, 1, 0, 2)
                taps(c, 1, 8, 16)
                gate_drain(c, 2)
                softplus(c, 1, 1, 3)
                head_low(c, 0)
                taps(c, 1, 16, 24)
                gate_drain(c, 3)
                taps(c, 1, 24, TAPS)
                head_low(c, 1)
            V.leave(4)

            dve.engine_nop().then_inc(conv_centred, 1)
            dve.wait_ge(mean_ready, 1)
            for c in range(CC):
                dve.scalar_tensor_tensor(out=conv_acc[:, c, :], in0=ps[:, 2, :], scalar=-1.0 / CONV, in1=conv_acc[:, c, :],
                                         op0=ALU.mult, op1=ALU.add).then_inc(conv_y, 1)
            norm(1, CONV, r_exp1)
            dve.wait_ge(row_copied, 2)
            for c in range(CC):
                tt(ln_y[:, c, :], conv_acc[:, c, :], ln_row[:, :], ALU.mult).then_inc(conv_y, 1)
            for c in range(CC):
                dve.wait_ge(split_hi, KC + c + 1)
                low(b_lo[:, c, :], ln_y[:, c, :], b_hi[:, c, :]).then_inc(split_lo, 1)

            with dve.Fori(0, 2) as i:
                V.enter(i, 4)
                for k in range(4):
                    j = i * 4 + k
                    dve.wait_ge(units_done, i * 4 + (U_BR + k + 1))
                    dve.wait_ge(sig_ready, i * 8 + (CC + 2 * k + 2))
                    V.do(dve.scalar_tensor_tensor(out=m1[:, k % 2, :], in0=ps[:, k, :], scalar=col("b_branch", j),
                                                  in1=chunk(g_lo8, j), op0=ALU.add, op1=ALU.mult))
                    tt(m2[:, k % 2, :], ps[:, 4 + k, :], chunk(g_hi8, j), ALU.mult).then_inc(br_drained, 1)
                    dve.wait_ge(br_drained, i * 4 + (CREDIT + k + 1))
                    tt(merged[:, k % 2, :], m1[:, k % 2, :], m2[:, k % 2, :], ALU.add).then_inc(x_new, 1)
                    dve.wait_ge(split_hi, i * 4 + (KC + CC + k + 1))
                    low(chunk(a_lo, j), merged[:, k % 2, :], chunk(a_hi, j)).then_inc(split_lo, 1)
            V.leave(2)

            def copy_tiles(dst, u_of, t_base):
                with dve.Fori(0, 2) as i:
                    for k in range(4):
                        dve.wait_ge(units_done, u_of(i, k))
                        dve.tensor_copy(chunk(dst, i * 4 + k), ps[:, k, :]).then_inc(tile_drained, 1)

            def new_residual(q, src, gain_post, gain_next, dst_hi, dst_lo, n_hi, r_exp):
                norm(q, D, r_exp)
                dve.wait_ge(row_copied, q + 1)

                def lows(c):
                    dve.wait_ge(split_hi, n_hi + c + 1)
                    low_scaled(dst_lo[:, c, :], resid[:, c, :], col(gain_next, c), dst_hi[:, c, :]).then_inc(split_lo, 1)

                for c in range(KC):
                    V.do(tt(src[:, c, :], src[:, c, :], scale_row[:, :], ALU.mult))
                    V.wait()
                    dve.scalar_tensor_tensor(out=resid[:, c, :], in0=src[:, c, :], scalar=col(gain_post, c),
                                             in1=resid[:, c, :], op0=ALU.mult, op1=ALU.add).then_inc(x_new, 1)
                    if c:
                        lows(c - 1)
                lows(KC - 1)
                norm(q + 1, D, r_exp)
                dve.wait_ge(row_copied, q + 2)

            copy_tiles(mix, lambda i, k: i * 4 + (U_WO + k + 1), T_WO)
            dve.wait_ge(x_again, 16)
            new_residual(2, mix, "g_mix_post", "g_ffn_pre", b_hi, b_lo, 2 * KC + CC, r_exp2)

            with dve.Fori(0, FC // 2) as i:
                for kk in range(2):
                    j = i * 2 + kk
                    drain(up_g[:, kk, :], None, i * 4 + (U_UP + 2 * kk), 2 * kk)
                    drain(up_u[:, kk, :], None, i * 4 + (U_UP + 2 * kk + 1), 2 * kk + 1)
                    dve.wait_ge(sig_ready, i * 2 + (CC + 2 * KC + kk + 1))
                    dve.wait_ge(tile_drained, i * 4 + (CREDIT + T_UP + 2 * kk + 2))
                    tt(up_h[:, kk, :], up_u[:, kk, :], up_s[:, kk, :], ALU.mult).then_inc(x_new, 1)
                    dve.wait_ge(split_hi, i * 2 + (3 * KC + CC + kk + 1))
                    low(chunk(h_lo, j), up_h[:, kk, :], chunk(h_hi, j)).then_inc(split_lo, 1)
            copy_tiles(ffo, lambda i, k: i * 12 + (U_DN + 3 * k + 3), T_DN)
            new_residual(4, ffo, "g_ffn_post", "g_2", a_hi, a_lo, 3 * KC + CC + FC, r_exp3)

            V.do(tt(lam_prod[:, 0, :], col("lambdas", 0, 64), col("lambdas", 64, 64), ALU.mult))
            V.do(tt(lam_prod[:, 1, :], col("lambdas", 128, 64), col("lambdas", 192, 64), ALU.mult))
            V.wait()
            dve.tensor_reduce(small[:, 0:2], lam_prod[:, :, :], AX.X, ALU.add).then_inc(lam_sum, 1)
            ts(small[:, 5:6], col("moba_q"), 0.125, ALU.mult)
            ts(small[:, 6:7], col("diff_q"), 0.125, ALU.mult)
            ts(small[:, 7:8], col("subln"), 1.0 - LAMBDA_INIT, ALU.mult)
            dve.wait_ge(lam_exp, 1)
            V.do(tt(small[:, 4:5], small[:, 3:4], small[:, 2:3], ALU.subtract))
            V.wait()
            V.do(ts(small[:, 4:5], small[:, 4:5], -LAMBDA_INIT, ALU.add))
            with dve.Fori(0, 4) as i:
                for k in range(4):
                    drain(chunk(y_qk, i * 4 + k), None, i * 4 + (U_Q2 + k), k)
            dve.wait_ge(ssq_ready, 1)
            ts(rows_v[:, :], ps[0:32, 4, :], 1.0 / 64, ALU.mult, EPS, ALU.add).then_inc(rows_var, 1)
            dve.wait_ge(rows_std, 1)
            V.do(dve.reciprocal(rows_y[:, :], rows_t[:, :]))
            V.wait()
            newton(rows_y[:, :], rows_v[:, :], rows_t[:, :])
            dve.engine_nop().then_inc(rows_ready, 1)
            dve.wait_ge(rows_hi_ready, 1)
            low(rows_lo[:, :], rows_y[:, :], rows_hi[:, :]).then_inc(rows_split, 1)
            for n in range(4):
                dve.wait_ge(units_done, U_V2 + 4)
                ts(v2_tok[:, n, 0:CONV], ps[:, n, :], ncol[:, 2, n:n + 1], ALU.mult).then_inc(tile_drained, 1)
            gains = [small[:, 5:6]] * 4 + [small[:, 6:7]] * 4 + [col("moba_k")] * 4 + [col("diff_k")] * 4
            for j in range(16):
                dve.wait_ge(nb_ready, j + 1)
                dve.scalar_tensor_tensor(out=y_qk[:, j, :], in0=ps[:, 6 + j % 2, :], scalar=gains[j], in1=y_qk[:, j, :],
                                         op0=ALU.mult, op1=ALU.mult).then_inc(nb_used, 1)
            for n in range(4):
                dve.wait_ge(units_done, U_V2 + 8)
                ts(v2_tok[:, n, CONV:2 * CONV], ps[:, n, :], ncol[:, 2, n:n + 1], ALU.mult).then_inc(tile_drained, 1)

            def biased(i, c, head):
                dve.wait_ge(s2_biased, i * 16 + (8 * c + 4 * head + 4))
                if c % 2 == 0:
                    slope = i * 2 + (8 + c + head)
                else:
                    slope = i + (16 + c // 2)
                slope = small[:, slope:slope + 1] if isinstance(slope, int) else small[:, bass.ds(slope, 1)]
                if head == 0 or c % 2 == 0:
                    V.do(ts(bias_h[:, :], dist[:, :], slope, ALU.mult))
                    V.wait()
                dve.wait_ge(s2_ready, i * 4 + (2 * c + head + 2))
                if not (isinstance(c, int) and isinstance(i, int) and i == 0 and c == 0):
                    dve.wait_ge(pt_ready, tq_of(i, c - 1) + (2 + (head if c % 2 else 0)))
                    dve.wait_ge(p2_exp, i * 4 + (2 * c + head - 1))
                V.do(dve.memset(small[:, 24:25], 0.0))
                for b in (3, 2, 0, 1):
                    w = slice(S_COL[b], S_COL[b] + (b + 1) * P)
                    dve.tensor_tensor_reduce(out=s2[:, head, w], in0=psf[:, 1024 + w.start:1024 + w.stop],
                                             in1=bias_h[:, (3 - b) * P:T], scale=1.0, scalar=-3.0e38,
                                             op0=ALU.add, op1=ALU.max,
                                             accum_out=smax[:, head, b:b + 1]).then_inc(s2_biased, 1)
                dve.wait_ge(s2_biased, i * 16 + (4 + 8 * c + 4 * head + 4))
                ts(neg_max[:, head, :], smax[:, head, :], -1.0, ALU.mult).then_inc(max_ready, 1)

            def normalised(i, c, head):
                dve.wait_ge(p2_exp, i * 4 + (2 * c + head + 1))
                V.do(dve.reciprocal(rden[:, head, :], den[:, head, :]))
                V.wait()
                if c % 2 and head:
                    V.do(ts(rden[:, 1, :], rden[:, 1, :], small[:, 4:5], ALU.mult))
                    V.wait()
                for b in (3, 2, 0, 1):
                    w = slice(S_COL[b], S_COL[b] + (b + 1) * P)
                    r = rden[:, head, b:b + 1]
                    if c % 2 == 0:
                        x = ts(s2[:, head, w], s2[:, head, w], r, ALU.mult)
                    elif head == 0:
                        V.do(ts(s2[:, 0, w], s2[:, 0, w], r, ALU.mult))
                    else:
                        x = dve.scalar_tensor_tensor(out=s2[:, 0, w], in0=s2[:, 1, w], scalar=r, in1=s2[:, 0, w],
                                                     op0=ALU.mult, op1=ALU.add)
                if c % 2 == 0 or head:
                    x.then_inc(p2_norm, 1)

            def low_probs(i, c, head):
                dve.wait_ge(pth_ready, tq_of(i, c) + (head + 1))
                low(pt_lo[:, :], psf[:, 5 * 512:5 * 512 + 1280], pt_hi[:, :]).then_inc(ptl_ready, 1)

            def gated(i, c):
                dve.wait_ge(gate_act, i * 2 + (c + 1))
                if not (isinstance(i, int) and c == 0):
                    dve.wait_ge(mixed_ready, i * 2 + c)
                dve.wait_ge(av2_ready, tq_of(i, c) + 3)
                tt(att2[:, :], ps[:, 1, :], gate_e[:, :], ALU.mult).then_inc(out_read, 1)

            def root(i, c):
                dve.wait_ge(drs_ready, i + (c // 2 + 1))
                V.do(tt(d_sq[:, :], d_y[:, :], d_y[:, :], ALU.mult))
                V.wait()
                V.do(dve.scalar_tensor_tensor(out=d_sq[:, :], in0=d_sq[:, :], scalar=-0.5, in1=d_v[:, :],
                                              op0=ALU.mult, op1=ALU.mult))
                V.wait()
                V.do(dve.scalar_tensor_tensor(out=d_y[:, :], in0=d_sq[:, :], scalar=1.5, in1=d_y[:, :],
                                              op0=ALU.add, op1=ALU.mult))
                V.wait()
                dve.scalar_tensor_tensor(out=att2[:, :], in0=att2[:, :], scalar=small[:, 7:8], in1=d_y[:, :],
                                         op0=ALU.mult, op1=ALU.mult).then_inc(d_final, 1)

            def dve_round(i, c, more=True):
                last = c - 1 if c else None
                if c % 2 == 0:
                    dve.wait_ge(av2_ready, tq_of(i, c) + 1)
                    V.do(dve.memset(v2_hi[:, :, 64:P].bitcast(F32), 0.0))
                    dve.memset(v2_lo[:, :, 64:P].bitcast(F32), 0.0).then_inc(gap_zeroed, 1)
                low_probs(i, c, 0)
                if last is not None and last % 2 == 0:
                    gated(i, last)
                if more:
                    biased(i, c + 1, 0)
                if last is not None and last % 2:
                    root(i, last)
                if c % 2:
                    dve.wait_ge(av2_ready, tq_of(i, c) + 2)
                    dve.wait_ge(mixed_ready, i * 2 + c)
                    dve.tensor_copy(att2[:, :], ps[:, 1, :]).then_inc(raw_copied, 1)
                if more:
                    if c % 2 == 0:
                        normalised(i, c + 1, 0)
                    biased(i, c + 1, 1)
                if c % 2 == 0:
                    low_probs(i, c, 1)
                if more and c % 2:
                    normalised(i, c + 1, 0)
                if c:
                    dve.wait_ge(gate_act, i * 2 + c)
                    if c % 2 == 0:
                        dve.wait_ge(att2_final, i + c // 2)
                dve.wait_ge(units_done, i * 2 + (U_G2 + c + 1))
                tt(gate[:, :], ps[:, 0, :], scale_row[:, :], ALU.mult).then_inc(tile_drained, 1)
                dve.wait_ge(tile_drained, i * 2 + (CREDIT + T_G2 + c + 1))
                ts(gate_e[:, :], gate[:, :], -80.0, ALU.max).then_inc(gate_clamped, 1)
                if c % 2:
                    dve.wait_ge(dss_ready, i + (c // 2 + 1))
                    ts(d_v[:, :], ps[:, 1, :], 1.0 / P, ALU.mult, EPS, ALU.add).then_inc(dvar_ready, 1)
                    dve.wait_ge(dvar_ready, i + (c // 2 + 1))
                    dve.memset(small[:, 25:26], 0.0).then_inc(out_read, 1)
                if more:
                    normalised(i, c + 1, 1)

            dve.wait_ge(dist_ready, 2)
            for head in range(2):
                biased(0, 0, head)
            for head in range(2):
                normalised(0, 0, head)
            dve_round(0, 0)
            with dve.Fori(0, 3) as i:
                V.enter(i, 20)
                dve_round(i, 1)
                dve_round(i, 2)
            V.leave(3)
            dve_round(0, 7, more=False)
            root(0, 7)

            with dve.Fori(0, 2) as i:
                for k in range(4):
                    dve.wait_ge(units_done, i * 4 + (U_W2 + k + 1))
                    tt(chunk(out_sb, i * 4 + k), ps[:, k, :], chunk(resid, i * 4 + k), ALU.add).then_inc(tile_drained, 1)

        @block.gpsimd
        def _(pool):
            def low_weights(n4, k, width=UNIT):
                pool.wait_ge(hi_ready, n4 * 4 + (k + 1))
                pool.tensor_tensor(w_lo[:, k % 2, 0:width], w_raw[:, k, 0:width], w_hi[:, k % 2, 0:width].bitcast(F32),
                                   ALU.subtract).then_inc(lo_ready, 1)

            def ahead(n4, k, width=UNIT):
                low_weights(n4 if k < 2 else n4 + 1, (k + 2) % 4, width)

            pool.sem_inc(spl_ready, 2)
            pool.memset(ones[:, :], 1.0).then_inc(consts, 1)
            pool.memset(ident[:, :], 0.0).then_inc(consts, 1)
            pool.memset(ident_bf[:, :], 0.0).then_inc(consts, 1)
            pool.memset(mask_bf[:, :], 0.0).then_inc(consts, 1)
            pool.memset(tri_f[:, :], -1.0).then_inc(consts, 1)
            pool.memset(neg_ones[:, :].bitcast(F32), -1.0).then_inc(consts, 1)
            pool.memset(head_sel[:, :], 0.0).then_inc(consts, 1)
            pool.wait_ge(consts, 7)
            for m in (ident, ident_bf):
                pool.affine_select(out=m[:, :], in_=m[:, :], compare_op=ALU.not_equal, fill=1.0, base=0,
                                   pattern=[[-1, P]], channel_multiplier=1).then_inc(consts, 1)
            pool.affine_select(out=mask_bf[:, :], in_=mask_bf[:, :], compare_op=ALU.is_gt, fill=NEG, base=0,
                               pattern=[[1, P]], channel_multiplier=-1).then_inc(consts, 1)
            pool.affine_select(out=tri_f[:, :], in_=tri_f[:, :], compare_op=ALU.is_ge, fill=0.0, base=0,
                               pattern=[[-1, P]], channel_multiplier=1).then_inc(consts, 1)
            pool.memset(u_pad[:, :, 0:TAPS - 1], 0.0)
            for h in range(8):
                pool.memset(small[:, 8 + h:9 + h], 2.0 ** -(h + 1))
            for h in range(4):
                pool.memset(small[:, 16 + h:17 + h], 2.0 ** (-2 * (h + 1)))
            pool.wait_ge(consts, 11)
            pool.tensor_copy(tri[:, :], tri_f[:, :]).then_inc(consts, 1)
            pool.wait_ge(consts, 12)
            pool.memset(head_sel[0:64, 30:31], 1.0).then_inc(consts, 1)
            pool.wait_ge(consts, 13)
            pool.memset(head_sel[64:P, 31:32], 1.0).then_inc(consts, 1)
            pool.wait_ge(consts, 14)

            low_weights(0, 0)
            low_weights(0, 1)
            with pool.Fori(0, 5) as i:
                for k in range(4):
                    ahead(i, k)

            def soft_low(c, half, g):
                w = slice(OU[half], OU[half] + WU[half])
                pool.wait_ge(sph_ready, c * 4 + (g + 1))
                pool.tensor_tensor(sp_lo[:, w], sp[:, w], sp_hi[:, w].bitcast(F32), ALU.subtract).then_inc(spl_ready, 1)

            def prob_low(c, half, g):
                w = slice(OU[half], OU[half] + WU[half])
                pool.wait_ge(pah_ready, c * 4 + (g + 1))
                pool.tensor_tensor(pa_lo[:, w], pa[:, w], pa_hi[:, w].bitcast(F32), ALU.subtract).then_inc(pal_ready, 1)

            with pool.Fori(0, 4) as c:
                soft_low(c, 0, 0)
                soft_low(c, 1, 1)
                ahead(c + 5, 0)
                prob_low(c, 0, 0)
                prob_low(c, 1, 1)
                soft_low(c, 0, 2)
                ahead(c + 5, 1)
                soft_low(c, 1, 3)
                ahead(c + 5, 2)
                prob_low(c, 0, 2)
                ahead(c + 5, 3)
                prob_low(c, 1, 3)
            with pool.Fori(U_BR // 4, U_DN // 4) as n4:
                for k in range(4):
                    ahead(n4, k)
            with pool.Fori(0, 2) as i:
                for k in range(4):
                    for r in range(DN_UNITS):
                        m = DN_UNITS * k + r
                        ahead(i * 3 + (U_DN // 4 + m // 4), m % 4, DN_CHUNKS[(r + 2) % 3] * P)
            with pool.Fori(U_Q2 // 4, U_V2 // 4) as n4:
                for k in range(4):
                    ahead(n4, k)
            pool.wait_ge(ssq_ready, 1)
            pool.iota(dist[:, :], pattern=[[1, T]], base=P - T, channel_multiplier=-1,
                      allow_small_or_imprecise_dtypes=True).then_inc(dist_ready, 1)
            pool.memset(sel_f[:, :, :], 0.0).then_inc(pool_step, 1)
            pool.wait_ge(dist_ready, 1)
            pool.affine_select(out=dist[:, :], in_=dist[:, :], compare_op=ALU.is_ge, fill=NEG, base=T - P,
                               pattern=[[-1, T]], channel_multiplier=1).then_inc(dist_ready, 1)
            pool.wait_ge(pool_step, 1)
            pool.affine_select(out=sel_f[:, :, :].rearrange("p j (h f) -> p j h f", h=2),
                               in_=sel_f[:, :, :].rearrange("p j (h f) -> p j h f", h=2),
                               compare_op=ALU.not_equal, fill=1.0, base=0, pattern=[[-2, 16], [-1, 2], [0, 64]],
                               channel_multiplier=1).then_inc(pool_step, 1)
            pool.wait_ge(pool_step, 2)
            pool.tensor_copy(sel_t[:, :, :], sel_f[:, :, :]).then_inc(sel_ready, 1)
            for k in range(6):
                ahead(U_V2 // 4 + k // 4, k % 4)

            def low_gate(i, m, slot=None):
                slot = m % 2 if slot is None else slot
                pool.wait_ge(hi_ready, i * 2 + (U_G2 + m + 1))
                pool.tensor_tensor(w_lo[:, m % 2, :], w_raw[:, slot, :], w_hi[:, m % 2, :].bitcast(F32),
                                   ALU.subtract).then_inc(lo_ready, 1)

            held = Steps(pool, pool_held)

            def hold():
                held.wait()
                held.do(pool.tensor_tensor(small[:, 28:29], small[:, 26:27], small[:, 27:28], ALU.add))

            def low_of(out, in0, high):
                return pool.tensor_tensor(out, in0, high.bitcast(F32), ALU.subtract)

            def stage_qk(i, c):
                j = chunk_of(i, c)
                for n, (dst, src, hi) in enumerate(((q2_lo, j, q2_hi), (k2_lo, j + 8, k2_hi))):
                    pool.wait_ge(qk2_hi, i * 4 + (2 * c + n + 1))
                    hold()
                    low_of(dst[:, :], chunk(y_qk, src), hi[:, :]).then_inc(qk2_lo, 1)

            def stage_v(i, c):
                j = chunk_of(i, c)
                w = slice(j * P, (j + 1) * P) if isinstance(j, int) else bass.ds(j * P, P)
                pool.wait_ge(v2_hi_ready, i * 2 + (c + 1))
                hold()
                dst, src = value_parts(c, v2_lo, v2_tok[:, :, w])
                high, _ = value_parts(c, v2_hi, v2_tok[:, :, w])
                low_of(dst, src, high).then_inc(v2_lo_ready, 1)

            def gate_silu(i, c):
                pool.wait_ge(gate_sig, i * 2 + (c + 1))
                pool.tensor_tensor(gate_e[:, :], gate[:, :], gate_e[:, :], ALU.mult).then_inc(gate_act, 1)

            def mixed_low(i, c):
                if c % 2:
                    pool.wait_ge(gate_act, i * 2 + (c + 1))
                    pool.wait_ge(d_final, i + (c // 2 + 1))
                    pool.tensor_tensor(att2[:, :], att2[:, :], gate_e[:, :], ALU.mult).then_inc(att2_final, 1)
                pool.wait_ge(split_hi, i * 2 + (4 * KC + CC + FC + c + 1))
                hold()
                j = chunk_of(i, c)
                low_of(chunk(b_lo, j), att2[:, :], chunk(b_hi, j)).then_inc(mixed_ready, 1)

            def pool_round(i, c, more=True):
                if more:
                    stage_qk(i, c + 1)
                if c:
                    gate_silu(i, c - 1)
                stage_v(i, c)
                if c:
                    mixed_low(i, c - 1)
                low_gate(i, c + 2)

            held.do(pool.memset(small[:, 26:28], 0.0))
            low_gate(0, 0)
            low_gate(0, 1)
            stage_qk(0, 0)
            pool_round(0, 0)
            with pool.Fori(0, 3) as i:
                held.enter(i, 8)
                pool_round(i, 1)
                pool_round(i, 2)
            held.leave(3)
            pool_round(0, 7, more=False)
            gate_silu(0, 7)
            mixed_low(0, 7)
            for m in range(2, 8):
                low_gate(0, 8 + m, slot=m % 4)


def _stream(w_in, w_conv_branch, w_att_branch, w_out, w_up, w_down, w_in_2, w_out_2):
    def tiles(w):
        k, n = w.shape
        return w.reshape(k // P, P, n // P, P).transpose(2, 1, 0, 3).reshape(n // P, P, k)

    def token_units(w):
        return w.reshape(4, 2, P, 512).transpose(0, 2, 1, 3).reshape(4, P, UNIT)

    t = tiles(w_in)
    v0 = 2 * CONV + 2 * 512
    glu = [t[x] for c in range(CC) for x in (c, CC + c)]
    qk = list(t[8:16])
    v = list(token_units(w_in[:, v0:v0 + 512]))
    g = [t[x] for c in range(4) for x in (20 + 2 * c, 21 + 2 * c, 28 + 2 * c, 29 + 2 * c)]
    tc, ta = tiles(w_conv_branch), tiles(w_att_branch)
    br = [np.concatenate([tc[j], ta[j]], axis=1) for j in range(KC)]
    wo = list(tiles(w_out))
    tu = tiles(w_up)
    up = [tu[x] for j in range(FC) for x in (j, FC + j)]
    dn = []
    for x in tiles(w_down):
        padded = np.zeros((P, DN_UNITS * UNIT), x.dtype)
        padded[:, :FC * P] = x
        dn += [padded[:, n * UNIT:(n + 1) * UNIT] for n in range(DN_UNITS)]
    t2 = tiles(w_in_2)
    q2 = [t2[x] for base in (0, 16, 4, 20) for x in range(base, base + 4)]
    v2 = list(token_units(w_in_2[:, 1024:1536])) + list(token_units(w_in_2[:, 3072:3584]))
    g2 = [t2[x] for i in range(4) for x in (12 + i, 28 + i)]
    w2 = list(tiles(w_out_2))
    units = glu + qk + v + g + br + wo + up + dn + q2 + v2 + g2 + w2
    assert len(units) == UNITS
    return np.ascontiguousarray(np.stack(units))


def kernel(**inputs):
    import concourse.bacc as _bacc
    from concourse.bass_utils import run_bass_kernel_spmd as _run

    a = {k: np.asarray(v) for k, v in inputs.items()}

    def rows(x):
        return x.reshape(-1, P).T

    conv_w = a["conv_dw_w"].reshape(TAPS, CC, P).transpose(2, 1, 0).reshape(P, CC * TAPS)
    lambdas = np.concatenate([a[n][0] for n in ("lambda_q1_2", "lambda_k1_2", "lambda_q2_2", "lambda_k2_2")])
    both = [np.concatenate([a[n][0], a[n][0]])[:, None] for n in ("moba_q_norm_2", "moba_k_norm_2", "diff_q_norm_2", "diff_k_norm_2")]
    vecs = np.ascontiguousarray(np.concatenate(
        [rows(a["norm_mix_pre"]), conv_w, rows(a["conv_dw_b"]), rows(a["conv_ln_g"]), rows(a["conv_ln_b"]),
         rows(a["b_conv_branch"]), rows(a["norm_mix_post"]), rows(a["norm_ffn_pre"]), rows(a["norm_ffn_post"]),
         rows(a["norm_g_2"][0]), *both, rows(a["diff_subln_2"][0]), np.zeros((P, 3), np.float32), np.broadcast_to(lambdas, (P, lambdas.size))], axis=1))
    arrays = {
        "x_t": np.ascontiguousarray(a["x"][0].T.reshape(KC, P, T).transpose(1, 0, 2)),
        "vecs": vecs,
        "weights": _stream(a["w_in"], a["w_conv_branch"], a["w_att_branch"], a["w_out"], a["w_ffn_up"], a["w_ffn_down"],
                           a["w_in_2"][0], a["w_out_2"][0]),
    }
    nc = _bacc.Bacc("TRN2", target_bir_lowering=False, num_devices=1)
    aps = [nc.dram_tensor(n, x.shape, mybir.dt.from_np(x.dtype), kind="ExternalInput").ap() for n, x in arrays.items()]
    out = nc.dram_tensor("out_t", (P, KC, T), F32, kind="ExternalOutput").ap()
    two_layer_block(nc, *aps, out)
    r = _run(nc, [arrays], core_ids=[0])
    got = r.results[0]["out_t"]
    return np.ascontiguousarray(got.transpose(1, 0, 2).reshape(D, T).T)[None]
```
